# Optimizing a Trainium2 kernel written in Bass

```python
import math
import jax
import jax.numpy as jnp
from jax import lax
import numpy as np

D_MODEL = 1024
BATCH = 1
SEQ = 1024
DEPTH = 1
DEC_BATCH = 8
DEC_SEQ = 1
PAST_LEN = 8192
PAGE_SIZE = 128

GLA_HEADS = 4
GLA_DK = 64
GLA_DV = 128
GLA_LOWRANK = 16
GLA_TAU = 16.0
GLA_CHUNK = 64
GLA_QK = GLA_HEADS * GLA_DK
GLA_V = GLA_HEADS * GLA_DV
ML_HEADS = 4
ML_D = 128
ML_CHUNK = 64
ML_W = ML_HEADS * ML_D
S5_GROUP = 16
S5_GROUPS = 32
S5_P = 64
S5_WIDTH = S5_GROUP * S5_GROUPS
MEM_LEN = 256
X_HEADS = 4
X_DH = D_MODEL // X_HEADS
D_FF = 2816
CONV_W = 3
EPS = 1e-6
NEG_BIG = -1e30
IN_SPLIT_SIZES = (GLA_QK, GLA_QK, GLA_V, GLA_V, GLA_LOWRANK,
                  ML_W, ML_W, ML_W, ML_W, ML_HEADS, ML_HEADS,
                  S5_WIDTH, D_MODEL, D_MODEL, D_MODEL)
W_IN_COLS = sum(IN_SPLIT_SIZES)

kernel_name = 'hybrid_gla_mlstm_s5_decoder_step'

def rmsnorm(x, g):
    xf = x.astype(jnp.float32)
    r = lax.rsqrt(jnp.mean(xf * xf, axis=-1, keepdims=True) + EPS)
    return (xf * r).astype(x.dtype) * g

def head_rmsnorm(x, g):
    B, T, H, d = x.shape
    r = lax.rsqrt(jnp.mean(x * x, axis=-1, keepdims=True) + EPS)
    return (x * r).reshape(B, T, H * d) * g

def split_in(z):
    idx = np.cumsum(IN_SPLIT_SIZES)[:-1].tolist()
    return jnp.split(z, idx, axis=-1)

def pad_time(x, L, value):
    pad = (-x.shape[1]) % L
    widths = [(0, 0), (0, pad)] + [(0, 0)] * (x.ndim - 2)
    return jnp.pad(x, widths, constant_values=value)

def to_chunks(x, L):
    B, Tp = x.shape[0], x.shape[1]
    x = x.reshape((B, Tp // L, L) + x.shape[2:])
    return jnp.moveaxis(x, (1, 3), (0, 2))

def from_chunks(o, T):
    o = jnp.moveaxis(o, (0, 2), (1, 3))
    B, nc, L = o.shape[:3]
    return o.reshape((B, nc * L) + o.shape[3:])[:, :T]

def gla_chunked(q, k, v, g, s0):
    T = q.shape[1]
    L = min(GLA_CHUNK, T)
    qc, kc, vc, gc = (to_chunks(pad_time(a, L, 0.0), L) for a in (q, k, v, g))
    mask = jnp.tril(jnp.ones((L, L), dtype=bool))

    def step(S, inp):
        qi, ki, vi, gi = inp
        b = jnp.cumsum(gi, axis=2)
        diff = b[:, :, :, None, :] - b[:, :, None, :, :]
        decay = jnp.exp(jnp.where(mask[:, :, None], diff, -jnp.inf))
        att = jnp.einsum('bhid,bhjd,bhijd->bhij', qi, ki, decay)
        o = (jnp.einsum('bhij,bhjv->bhiv', att, vi)
             + jnp.einsum('bhid,bhdv->bhiv', qi * jnp.exp(b), S))
        b_end = b[:, :, -1]
        k_dec = ki * jnp.exp(b_end[:, :, None, :] - b)
        S_new = jnp.exp(b_end)[..., None] * S + jnp.einsum('bhjd,bhjv->bhdv', k_dec, vi)
        return S_new, o

    S_fin, o = lax.scan(step, s0, (qc, kc, vc, gc))
    return from_chunks(o, T), S_fin

def mlstm_chunked(q, k, v, log_i, log_f, c0, n0, m0):
    T = q.shape[1]
    L = min(ML_CHUNK, T)
    qc, kc, vc = (to_chunks(pad_time(a, L, 0.0), L) for a in (q, k, v))
    ic = to_chunks(pad_time(log_i, L, NEG_BIG), L)
    fc = to_chunks(pad_time(log_f, L, 0.0), L)
    mask = jnp.tril(jnp.ones((L, L), dtype=bool))

    def step(carry, inp):
        C, n, m = carry
        qi, ki, vi, li, lf = inp
        b = jnp.cumsum(lf, axis=-1)
        w_inter = b + m[..., None]
        w_intra = jnp.where(mask, b[..., :, None] - b[..., None, :] + li[..., None, :], -jnp.inf)
        m_tok = jnp.maximum(w_inter, jnp.max(w_intra, axis=-1))
        a_inter = jnp.exp(w_inter - m_tok)
        s = jnp.einsum('bhid,bhjd->bhij', qi, ki) * jnp.exp(w_intra - m_tok[..., None])
        num = (jnp.einsum('bhij,bhjv->bhiv', s, vi)
               + a_inter[..., None] * jnp.einsum('bhid,bhdv->bhiv', qi, C))
        den = jnp.sum(s, axis=-1) + a_inter * jnp.einsum('bhid,bhd->bhi', qi, n)
        h = num / jnp.maximum(jnp.abs(den), jnp.exp(-m_tok))[..., None]
        b_end = b[..., -1]
        w_end_inter = b_end + m
        w_end = b_end[..., None] - b + li
        m_new = jnp.maximum(w_end_inter, jnp.max(w_end, axis=-1))
        e_inter = jnp.exp(w_end_inter - m_new)
        e_j = jnp.exp(w_end - m_new[..., None])
        C_new = e_inter[..., None, None] * C + jnp.einsum('bhj,bhjd,bhjv->bhdv', e_j, ki, vi)
        n_new = e_inter[..., None] * n + jnp.einsum('bhj,bhjd->bhd', e_j, ki)
        return (C_new, n_new, m_new), h

    (C, n, m), h = lax.scan(step, (c0, n0, m0), (qc, kc, vc, ic, fc))
    return from_chunks(h, T), C, n, m

def s5_ssm(u, h0_re, h0_im, lam_re, lam_im, log_dt, b_re, b_im, c_re, c_im, d, w_glu):
    B, T, _ = u.shape
    ug = u.reshape(B, T, S5_GROUPS, S5_GROUP)
    dt = jnp.exp(log_dt)[:, None]
    mag = jnp.exp(lam_re * dt)
    lb_re = mag * jnp.cos(lam_im * dt)
    lb_im = mag * jnp.sin(lam_im * dt)
    nr = lb_re - 1.0
    den = lam_re * lam_re + lam_im * lam_im
    f_re = (nr * lam_re + lb_im * lam_im) / den
    f_im = (lb_im * lam_re - nr * lam_im) / den
    bb_re = f_re[..., None] * b_re - f_im[..., None] * b_im
    bb_im = f_re[..., None] * b_im + f_im[..., None] * b_re
    bu_re = jnp.einsum('btgc,gpc->btgp', ug, bb_re)
    bu_im = jnp.einsum('btgc,gpc->btgp', ug, bb_im)
    bu_re = bu_re.at[:, 0].add(lb_re * h0_re - lb_im * h0_im)
    bu_im = bu_im.at[:, 0].add(lb_re * h0_im + lb_im * h0_re)
    a_re = jnp.broadcast_to(lb_re, bu_re.shape)
    a_im = jnp.broadcast_to(lb_im, bu_im.shape)

    def combine(e1, e2):
        a1r, a1i, b1r, b1i = e1
        a2r, a2i, b2r, b2i = e2
        return (a1r * a2r - a1i * a2i, a1r * a2i + a1i * a2r,
                a2r * b1r - a2i * b1i + b2r, a2r * b1i + a2i * b1r + b2i)

    _, _, hr, hi = lax.associative_scan(combine, (a_re, a_im, bu_re, bu_im), axis=1)
    y = (jnp.einsum('btgp,gcp->btgc', hr, c_re) - jnp.einsum('btgp,gcp->btgc', hi, c_im)
         + d.reshape(S5_GROUPS, S5_GROUP) * ug).reshape(B, T, S5_WIDTH)
    y = jax.nn.gelu(y)
    y = y * jax.nn.sigmoid(y @ w_glu)
    return y, hr[:, -1], hi[:, -1]

def mixer_block(hn, s_gla, s_c, s_n, s_m, s_re, s_im, P, l):
    B, T, _ = hn.shape
    f32 = jnp.float32
    (gq, gk, gv, gr, ga, mq, mk, mv, mo, mi, mf, su, za, zb, zc) = split_in(hn @ P['w_in'][l])
    q = gq.astype(f32).reshape(B, T, GLA_HEADS, GLA_DK) * GLA_DK ** -0.5
    k = gk.astype(f32).reshape(B, T, GLA_HEADS, GLA_DK)
    v = gv.astype(f32).reshape(B, T, GLA_HEADS, GLA_DV)
    a_pre = (ga @ P['w_gla_alpha'][l] + P['b_gla_alpha'][l]).astype(f32)
    g = (jax.nn.log_sigmoid(a_pre) / GLA_TAU).reshape(B, T, GLA_HEADS, GLA_DK)
    o_a, s_gla_new = gla_chunked(q, k, v, g, s_gla.astype(f32))
    y_a = head_rmsnorm(o_a, P['gla_head_norm'][l]) * jax.nn.silu(gr.astype(f32))
    q = mq.astype(f32).reshape(B, T, ML_HEADS, ML_D) * ML_D ** -0.5
    k = mk.astype(f32).reshape(B, T, ML_HEADS, ML_D)
    v = mv.astype(f32).reshape(B, T, ML_HEADS, ML_D)
    log_i = (mi + P['b_mlstm_i'][l]).astype(f32)
    log_f = jax.nn.log_sigmoid((mf + P['b_mlstm_f'][l]).astype(f32))
    h_b, c_new, n_new, m_new = mlstm_chunked(q, k, v, log_i, log_f, s_c.astype(f32),
                                             s_n.astype(f32), s_m.astype(f32))
    y_b = head_rmsnorm(h_b, P['mlstm_head_norm'][l]) * jax.nn.sigmoid(mo.astype(f32))
    y_c, re_new, im_new = s5_ssm(su.astype(f32), s_re.astype(f32), s_im.astype(f32),
                                 P['s5_lam_re'][l], P['s5_lam_im'][l], P['s5_log_dt'][l],
                                 P['s5_b_re'][l], P['s5_b_im'][l], P['s5_c_re'][l],
                                 P['s5_c_im'][l], P['s5_d'][l], P['s5_w_glu'][l])
    dt = hn.dtype
    merged = (jax.nn.sigmoid(za) * (y_a.astype(dt) @ P['w_branch_a'][l])
              + jax.nn.sigmoid(zb) * (y_b.astype(dt) @ P['w_branch_b'][l])
              + jax.nn.sigmoid(zc) * (y_c.astype(dt) @ P['w_branch_c'][l]))
    return merged @ P['w_out'][l], (s_gla_new, c_new, n_new, m_new, re_new, im_new)

def memory_kv(mem, g, w_k, w_v):
    B, M, _ = mem.shape
    mn = rmsnorm(mem, g)
    return ((mn @ w_k).reshape(B, M, X_HEADS, X_DH), (mn @ w_v).reshape(B, M, X_HEADS, X_DH))

def cross_attn(hn, mk, mv, w_q, w_o):
    B, T, _ = hn.shape
    q = (hn @ w_q).reshape(B, T, X_HEADS, X_DH)
    s = jnp.einsum('bthd,bmhd->bhtm', q, mk).astype(jnp.float32) * X_DH ** -0.5
    p = jax.nn.softmax(s, axis=-1).astype(mv.dtype)
    o = jnp.einsum('bhtm,bmhd->bthd', p, mv).reshape(B, T, D_MODEL)
    return o @ w_o

def conv_ffn(hn, buf, w_up, conv_w, conv_b, w_down):
    T = hn.shape[1]
    up = hn @ w_up
    full = jnp.concatenate([buf.astype(up.dtype), up], axis=1)
    conv = sum(full[:, j:j + T] * conv_w[j] for j in range(CONV_W)) + conv_b
    a, gt = jnp.split(conv, 2, axis=-1)
    return (a * jax.nn.silu(gt)) @ w_down, full[:, T:]

def run_trunk(x, mem_k, mem_v, states, P):
    new_states = []
    for l in range(DEPTH):
        s_gla, s_c, s_n, s_m, s_re, s_im, s_conv = states[l]
        y, mix_state = mixer_block(rmsnorm(x, P['norm_mix'][l]), s_gla, s_c, s_n, s_m, s_re, s_im, P, l)
        x = x + y
        x = x + cross_attn(rmsnorm(x, P['norm_cross'][l]), mem_k[l], mem_v[l], P['w_cq'][l], P['w_co'][l])
        f, conv_state = conv_ffn(rmsnorm(x, P['norm_ffn'][l]), s_conv, P['w_ffn_up'][l],
                                 P['ffn_conv_w'][l], P['ffn_conv_b'][l], P['w_ffn_down'][l])
        x = x + f
        new_states.append(mix_state + (conv_state,))
    y = rmsnorm(x, P['norm_final'])
    stacked = [jnp.stack([new_states[l][i] for l in range(DEPTH)]) for i in range(7)]
    return y, stacked

def setup_inputs(seed: int = 0) -> dict:
    key = jax.random.key(seed)
    keys = list(jax.random.split(key, 64))
    f32 = jnp.float32

    def nrm(shape, scale):
        return jax.random.normal(keys.pop(), shape, f32) * scale

    def gain(shape):
        return 1.0 + 0.02 * jax.random.normal(keys.pop(), shape, f32)

    modes = jnp.arange(S5_P, dtype=f32)
    return {
        'x_prompt': nrm((BATCH, SEQ, D_MODEL), 1.0),
        'x_sample': nrm((DEC_BATCH, DEC_SEQ, D_MODEL), 1.0),
        'mem_prompt': nrm((BATCH, MEM_LEN, D_MODEL), 1.0),
        'cache_mem_k': nrm((DEPTH, DEC_BATCH, MEM_LEN, X_HEADS, X_DH), 1.0),
        'cache_mem_v': nrm((DEPTH, DEC_BATCH, MEM_LEN, X_HEADS, X_DH), 1.0),
        'state_gla': nrm((DEPTH, DEC_BATCH, GLA_HEADS, GLA_DK, GLA_DV), 0.5),
        'state_mlstm_c': nrm((DEPTH, DEC_BATCH, ML_HEADS, ML_D, ML_D), 0.5),
        'state_mlstm_n': nrm((DEPTH, DEC_BATCH, ML_HEADS, ML_D), 0.5),
        'state_mlstm_m': nrm((DEPTH, DEC_BATCH, ML_HEADS), 1.0),
        'state_s5_re': nrm((DEPTH, DEC_BATCH, S5_GROUPS, S5_P), 0.1),
        'state_s5_im': nrm((DEPTH, DEC_BATCH, S5_GROUPS, S5_P), 0.1),
        'state_ffn_conv': nrm((DEPTH, DEC_BATCH, CONV_W - 1, 2 * D_FF), 1.0),
        'norm_mix': gain((DEPTH, D_MODEL)),
        'w_in': nrm((DEPTH, D_MODEL, W_IN_COLS), D_MODEL ** -0.5),
        'w_gla_alpha': nrm((DEPTH, GLA_LOWRANK, GLA_QK), GLA_LOWRANK ** -0.5),
        'b_gla_alpha': nrm((DEPTH, GLA_QK), 0.1),
        'gla_head_norm': gain((DEPTH, GLA_V)),
        'b_mlstm_i': nrm((DEPTH, ML_HEADS), 0.1),
        'b_mlstm_f': jnp.linspace(3.0, 6.0, ML_HEADS, dtype=f32)[None, :] + nrm((DEPTH, ML_HEADS), 0.1),
        'mlstm_head_norm': gain((DEPTH, ML_W)),
        's5_lam_re': -0.5 + nrm((DEPTH, S5_GROUPS, S5_P), 0.01),
        's5_lam_im': math.pi * modes + nrm((DEPTH, S5_GROUPS, S5_P), 0.01),
        's5_log_dt': jax.random.uniform(keys.pop(), (DEPTH, S5_GROUPS), f32, math.log(1e-3), math.log(1e-1)),
        's5_b_re': nrm((DEPTH, S5_GROUPS, S5_P, S5_GROUP), (2 * S5_GROUP) ** -0.5),
        's5_b_im': nrm((DEPTH, S5_GROUPS, S5_P, S5_GROUP), (2 * S5_GROUP) ** -0.5),
        's5_c_re': nrm((DEPTH, S5_GROUPS, S5_GROUP, S5_P), S5_P ** -0.5),
        's5_c_im': nrm((DEPTH, S5_GROUPS, S5_GROUP, S5_P), S5_P ** -0.5),
        's5_d': nrm((DEPTH, S5_WIDTH), 1.0),
        's5_w_glu': nrm((DEPTH, S5_WIDTH, S5_WIDTH), S5_WIDTH ** -0.5),
        'w_branch_a': nrm((DEPTH, GLA_V, D_MODEL), GLA_V ** -0.5),
        'w_branch_b': nrm((DEPTH, ML_W, D_MODEL), ML_W ** -0.5),
        'w_branch_c': nrm((DEPTH, S5_WIDTH, D_MODEL), S5_WIDTH ** -0.5),
        'w_out': nrm((DEPTH, D_MODEL, D_MODEL), D_MODEL ** -0.5),
        'norm_cross': gain((DEPTH, D_MODEL)),
        'norm_mem': gain((DEPTH, D_MODEL)),
        'w_cq': nrm((DEPTH, D_MODEL, D_MODEL), D_MODEL ** -0.5),
        'w_ck': nrm((DEPTH, D_MODEL, D_MODEL), D_MODEL ** -0.5),
        'w_cv': nrm((DEPTH, D_MODEL, D_MODEL), D_MODEL ** -0.5),
        'w_co': nrm((DEPTH, D_MODEL, D_MODEL), D_MODEL ** -0.5),
        'norm_ffn': gain((DEPTH, D_MODEL)),
        'w_ffn_up': nrm((DEPTH, D_MODEL, 2 * D_FF), D_MODEL ** -0.5),
        'ffn_conv_w': nrm((DEPTH, CONV_W, 2 * D_FF), CONV_W ** -0.5),
        'ffn_conv_b': nrm((DEPTH, 2 * D_FF), 0.02),
        'w_ffn_down': nrm((DEPTH, D_FF, D_MODEL), D_FF ** -0.5),
        'norm_final': gain((D_MODEL,)),
    }

def reference(x_prompt, x_sample, mem_prompt, cache_mem_k, cache_mem_v, state_gla, state_mlstm_c,
              state_mlstm_n, state_mlstm_m, state_s5_re, state_s5_im, state_ffn_conv,
              norm_mix, w_in, w_gla_alpha, b_gla_alpha, gla_head_norm, b_mlstm_i, b_mlstm_f,
              mlstm_head_norm, s5_lam_re, s5_lam_im, s5_log_dt, s5_b_re, s5_b_im, s5_c_re, s5_c_im,
              s5_d, s5_w_glu, w_branch_a, w_branch_b, w_branch_c, w_out, norm_cross, norm_mem,
              w_cq, w_ck, w_cv, w_co, norm_ffn, w_ffn_up, ffn_conv_w, ffn_conv_b, w_ffn_down,
              norm_final):
    P = dict(norm_mix=norm_mix, w_in=w_in, w_gla_alpha=w_gla_alpha, b_gla_alpha=b_gla_alpha,
             gla_head_norm=gla_head_norm, b_mlstm_i=b_mlstm_i, b_mlstm_f=b_mlstm_f,
             mlstm_head_norm=mlstm_head_norm, s5_lam_re=s5_lam_re, s5_lam_im=s5_lam_im,
             s5_log_dt=s5_log_dt, s5_b_re=s5_b_re, s5_b_im=s5_b_im, s5_c_re=s5_c_re,
             s5_c_im=s5_c_im, s5_d=s5_d, s5_w_glu=s5_w_glu, w_branch_a=w_branch_a,
             w_branch_b=w_branch_b, w_branch_c=w_branch_c, w_out=w_out, norm_cross=norm_cross,
             w_cq=w_cq, w_co=w_co, norm_ffn=norm_ffn, w_ffn_up=w_ffn_up, ffn_conv_w=ffn_conv_w,
             ffn_conv_b=ffn_conv_b, w_ffn_down=w_ffn_down, norm_final=norm_final)
    f32 = jnp.float32
    Bp = x_prompt.shape[0]
    zero_state = (jnp.zeros((Bp, GLA_HEADS, GLA_DK, GLA_DV), f32),
                  jnp.zeros((Bp, ML_HEADS, ML_D, ML_D), f32),
                  jnp.zeros((Bp, ML_HEADS, ML_D), f32),
                  jnp.zeros((Bp, ML_HEADS), f32),
                  jnp.zeros((Bp, S5_GROUPS, S5_P), f32),
                  jnp.zeros((Bp, S5_GROUPS, S5_P), f32),
                  jnp.zeros((Bp, CONV_W - 1, 2 * D_FF), x_prompt.dtype))
    mem_kv = [memory_kv(mem_prompt, norm_mem[l], w_ck[l], w_cv[l]) for l in range(DEPTH)]
    p_mem_k = jnp.stack([kv[0] for kv in mem_kv])
    p_mem_v = jnp.stack([kv[1] for kv in mem_kv])
    y_prompt, (p_gla, p_c, p_n, p_m, p_re, p_im, p_conv) = run_trunk(
        x_prompt, p_mem_k, p_mem_v, [zero_state] * DEPTH, P)
    sample_states = [(state_gla[l], state_mlstm_c[l], state_mlstm_n[l], state_mlstm_m[l],
                      state_s5_re[l], state_s5_im[l], state_ffn_conv[l]) for l in range(DEPTH)]
    y_sample, (s_gla, s_c, s_n, s_m, s_re, s_im, s_conv) = run_trunk(
        x_sample, cache_mem_k, cache_mem_v, sample_states, P)
    return (y_prompt, y_sample, p_gla, p_c, p_n, p_m, p_re, p_im, p_conv, p_mem_k, p_mem_v,
            s_gla, s_c, s_n, s_m, s_re, s_im, s_conv)


_drawn_inputs = setup_inputs


def setup_inputs(seed=0):
    import zlib

    import numpy as np

    out = dict(_drawn_inputs(seed))
    spreads = {}
    factors = {'gla_head_norm': 8.0,
     'mlstm_head_norm': 8.0,
     's5_lam_re': 16.528,
     's5_c_re': 3.617,
     's5_c_im': 9.311,
     'norm_cross': 8.0,
     'norm_mem': 2.925,
     'norm_ffn': 2.821,
     'ffn_conv_b': 4.197,
     'norm_final': 7.913}
    for name, (base, spread) in spreads.items():
        noise = np.random.default_rng([zlib.crc32(name.encode()), seed]).standard_normal(out[name].shape)
        drawn = base * np.exp(spread * noise) if base else spread * noise
        out[name] = jnp.asarray(drawn.astype(out[name].dtype))
    for name, factor in factors.items():
        out[name] = (out[name] * factor).astype(out[name].dtype)
    return out
```

```python
import concourse.bass as bass
from concourse import mybir
from contextlib import ExitStack
import math
import numpy as np

F32 = mybir.dt.float32
F32R = mybir.dt.float32r
U8 = mybir.dt.uint8
ACT = mybir.ActivationFunctionType
ALU = mybir.AluOpType
AX = mybir.AxisListType

D = 1024
T = 1024
B = 8
N = T + B
TG, NTG = 344, 3
KT = D // 128
CH, NCH = 128, T // 128
FF = 2816
NF = FF // 128
MEM = 256
EPS = 1e-6
NEG = -1.0e30
LEVELS = 8

SL_CK, SL_CV = 0, 8
SL_SPECIAL = 16
SL_SU = 17
SL_MQ, SL_MKV = 21, 25
SL_MO = 33
SL_GQ, SL_GKV = 37, 39
SL_GR = 45
SL_GATE = 49
SL_OUT = SL_GATE + 36
SL_CQ, SL_CO = SL_OUT + 8, SL_OUT + 16
SL_FFN = SL_OUT + 24
N_SLABS = SL_FFN + 6 * (NF // 2)
G_SPECIAL, G_SU = 16, 17
GR_GLU = 21
G_MQ, G_MKV, G_MO = 25, 29, 37
G_GQ, G_GKV, G_GR = 41, 43, 49
G_GATE = 53
G_OUT = G_GATE + 48
G_CQ, G_CO = G_OUT + 8, G_OUT + 16
G_FFN = G_OUT + 24

BASE = 16512
O_XH = BASE
O_XL = O_XH + KT * N * 4
O_WRAW = O_XL + KT * N * 4
O_WH = O_WRAW + 8192
O_WL = O_WH + 8192
O_WPL = O_WL + 8192
O_TMP = O_WPL + 4096
O_RB = O_TMP + 2 * N * 4
O_GT = O_RB + N * 4
O_ROWS = O_GT + N * 4
O_CST = O_ROWS + N * 4
CST_BYTES = 6144
O_ARENA = O_CST + CST_BYTES
ARENA = (229344 - O_ARENA) // 4


class Steps:

    def __init__(self, eng, sem):
        self.eng, self.sem, self.n = eng, sem, 0
        self.i, self.per = None, 0

    def enter(self, i, per):
        self.i, self.per, self.first = i, per, self.n

    def leave(self, times):
        assert self.n == self.first + self.per
        self.n, self.i = self.first + self.per * times, None

    def link(self, ins):
        self.n = self.n + 1
        ins.then_inc(self.sem, 1)
        self.eng.wait_ge(self.sem, self.n if self.i is None else self.i * self.per + self.n)
        return ins


def counts(*steps):
    return lambda name, times: (times - 1) * len(steps) + steps.index(name) + 1


def program(nc, I, O):
    ctx = ExitStack()
    with ctx:
        def sem(name):
            return ctx.enter_context(nc.semaphore(name))

        def at(name, shape, off, dt=F32):
            return nc.alloc_sbuf_tensor_at(name, shape, dt, offset=off)

        ctx.enter_context(nc.sbuf_tensor("fence", [128, (229344 - BASE) // 4], F32))
        ps = ctx.enter_context(nc.psum_tensor("ps", [128, 8, 512], F32))

        XH = at("XH", [128, KT, N], O_XH, F32R)
        XL = at("XL", [128, KT, N], O_XL, F32R)
        WRAW = at("WRAW", [128, 2, 8, 128], O_WRAW)
        WH = at("WH", [128, 2, 8, 128], O_WH, F32R)
        WL = at("WL", [128, 2, 8, 128], O_WL, F32R)
        WPL = at("WPL", [128, 2, 4, 128], O_WPL)
        TMP = at("TMP", [128, 2, N], O_TMP)
        RB = at("RB", [128, N], O_RB)
        GT = at("GT", [128, N], O_GT)
        ROWS = at("ROWS", [128, N], O_ROWS)

        o = [O_CST]

        def cst(name, shape, dt=F32, size=4):
            t = at(name, shape, o[0], dt)
            o[0] += (math.prod(shape[1:]) * size + 31) // 32 * 32
            assert o[0] <= O_ARENA
            return t

        CF = cst("CF", [128, 5, 128])
        IDENT, MASKNEG, ONES, PSW = (CF[:, k, :] for k in (0, 2, 3, 4))
        SHIFT = CF[:, 0:2, :].rearrange("p a i -> p (a i)")
        LVL = cst("LVL", [128, LEVELS, 128], U8, 1)
        SC = cst("SC", [128, 64])
        GAIN = SC[:, 0:40].rearrange("p (a b) -> p a b", b=8)
        BALPHA, GLAN, MLN, S5D = SC[:, 40:42], SC[:, 42:46], SC[:, 46:50], SC[:, 50:54]
        SGN, EPSC, BIF, NSGN = SC[:, 54:55], SC[:, 55:56], SC[:, 56:57], SC[:, 57:58]
        WALPHA = cst("WALPHA", [16, 256])
        NRM = cst("NRM", [128, 16])

        def area(name, shape, first, dt=F32):
            assert first + math.prod(shape[1:]) <= ARENA, (name, first + math.prod(shape[1:]), ARENA)
            return at(name, shape, O_ARENA + 4 * first, dt)

        def acc(slot):
            return ps[:, 3 * slot:3 * slot + 3, 0:TG]

        def t3(ap):
            return ap.rearrange("p (a b) -> p a b", b=TG)

        def two(k):
            return ps[:, k:k + 2, :].rearrange("p a (c i) -> p (a c) i", i=128)

        consts_in = sem("consts_in")
        w_loaded = [sem("w_loaded0"), sem("w_loaded1")]
        w_hi, w_lo = sem("w_hi"), sem("w_lo")
        wp_loaded = [sem("wp_loaded0"), sem("wp_loaded1")]
        acc_ready, acc_free = sem("acc_ready"), [sem("acc_free0"), sem("acc_free1")]
        sq_ready, norm_dve, norm_pe, norm_act = sem("sq_ready"), sem("norm_dve"), sem("norm_pe"), sem("norm_act")
        xn_ready, xh_ready, xl_ready = sem("xn_ready"), sem("xh_ready"), sem("xl_ready")
        act_step, dve_step = sem("act_step"), sem("dve_step")

        block = ctx.enter_context(nc.Block())

        def evacuated(eng, groups):
            eng.wait_ge(acc_free[0], (groups + 1) // 2)
            eng.wait_ge(acc_free[1], groups // 2)

        def sp_weights(sp):
            sp.dma_start(WRAW[:, 0], I["wslabs"][0]).then_inc(w_loaded[0], 16)
            sp.dma_start(WRAW[:, 1], I["wslabs"][1]).then_inc(w_loaded[1], 16)
            sp.wait_ge(w_lo, 1)
            sp.dma_start(WRAW[:, 0], I["wslabs"][2]).then_inc(w_loaded[0], 16)
            with sp.Fori(0, (N_SLABS - 3) // 2) as i:
                for s in range(2):
                    sp.wait_ge(w_lo, i * 2 + s + 2)
                    src = I["wslabs"][bass.ds(i * 2 + s + 3, 1)].rearrange("a p k m -> (a p) k m")
                    sp.dma_start(WRAW[:, (s + 1) % 2], src).then_inc(w_loaded[(s + 1) % 2], 16)

        def act_hi(act, n, slot, loaded, done):
            act.wait_ge(w_loaded[slot], loaded)
            if done is not None:
                act.wait_ge(acc_ready, done)
            nc.scalar.activation(WH[:, slot], WRAW[:, slot], ACT.Copy).then_inc(w_hi, 1)

        def dve_lo(dve, n, slot):
            dve.wait_ge(w_hi, n + 1)
            nc.vector.tensor_tensor(WL[:, slot], WRAW[:, slot], WH[:, slot].bitcast(F32),
                                    ALU.subtract).then_inc(w_lo, 1)

        def split_product(pe, out, slot, xh, xl, k0, nk, step=1):
            for k in range(nk):
                w = k0 + k * step
                for t in range(len(out)):
                    pe.matmul(out[t], WH[:, slot, w, :], xh(k, t), start=(k == 0), stop=False)
                    pe.matmul(out[t], WH[:, slot, w, :], xl(k, t), start=False, stop=False)
                for t in range(len(out)):
                    last = pe.matmul(out[t], WL[:, slot, w, :], xh(k, t), start=False, stop=(k == nk - 1))
            return last

        def xh_cols(k, t):
            return XH[:, k, t * TG:(t + 1) * TG]

        def xl_cols(k, t):
            return XL[:, k, t * TG:(t + 1) * TG]

        def banks(slot):
            return [ps[:, 3 * slot + t, 0:TG] for t in range(NTG)]

        def pe_project(pe, n0, g0, count):
            def one(n, free, slot, gslot):
                pe.wait_ge(w_lo, n + 1)
                pe.wait_ge(acc_free[gslot], free)
                split_product(pe, banks(gslot), slot, xh_cols, xl_cols, 0, KT).then_inc(acc_ready, 1)
            if count > 1:
                with pe.Fori(0, count // 2) as i:
                    for s in range(2):
                        one(i * 2 + (n0 + s), i + (g0 + s) // 2, (n0 + s) % 2, (g0 + s) % 2)
            if count % 2:
                one(n0 + count - 1, (g0 + count - 1) // 2, (n0 + count - 1) % 2, (g0 + count - 1) % 2)

        def act_project(act, n0, g0, count, dst, z0, scale=1.0):
            def one(n, g, slot, gslot, z, half):
                act.wait_ge(acc_ready, g + 1)
                nc.scalar.activation(t3(dst[:, bass.ts(z, N)]), acc(gslot), ACT.Copy,
                                     scale=scale).then_inc(acc_free[gslot], 1)
                act_hi(act, n + 2, slot, half, None)
            if count > 1:
                with act.Fori(0, count // 2) as i:
                    for s in range(2):
                        one(i * 2 + (n0 + s), i * 2 + (g0 + s), (n0 + s) % 2, (g0 + s) % 2,
                            i * 2 + (z0 + s), i * 16 + 16 * ((n0 + s) // 2 + 2))
            if count % 2:
                c = count - 1
                one(n0 + c, g0 + c, (n0 + c) % 2, (g0 + c) % 2, z0 + c, 16 * ((n0 + c) // 2 + 2))

        def dve_project(dve, n0, count):
            if count > 1:
                with dve.Fori(0, count // 2) as i:
                    for s in range(2):
                        dve_lo(dve, i * 2 + (n0 + s + 2), (n0 + s) % 2)
            if count % 2:
                dve_lo(dve, n0 + count + 1, (n0 + count - 1) % 2)

        def pe_first(pe, n0, g0, ks):
            pe.wait_ge(w_lo, n0 + 2)
            pe.wait_ge(acc_free[0], (g0 + 1) // 2)
            pe.wait_ge(acc_free[1], g0 // 2)
            for k in range(KT):
                pe.wait_ge(xl_ready, KT * ks + k + 1)
                for s in range(2):
                    slot, out = (n0 + s) % 2, banks((g0 + s) % 2)
                    for t in range(NTG):
                        pe.matmul(out[t], WH[:, slot, k, :], xh_cols(k, t), start=(k == 0), stop=False)
                        pe.matmul(out[t], WH[:, slot, k, :], xl_cols(k, t), start=False, stop=False)
                    for t in range(NTG):
                        last = pe.matmul(out[t], WL[:, slot, k, :], xh_cols(k, t), start=False, stop=(k == KT - 1))
                    if k == KT - 1:
                        last.then_inc(acc_ready, 1)

        SS = GT

        def act_square(act, done, count, tile, slot, width):
            if done is not None:
                act.wait_ge(norm_dve, done)
            nc.scalar.activation(TMP[:, slot, 0:width], tile, ACT.Square).then_inc(sq_ready, 1)

        def dve_sum(dve, count, first, slot, width, before):
            dve.wait_ge(sq_ready, count + 1)
            if first:
                nc.vector.tensor_copy(SS[:, 0:width], TMP[:, slot, 0:width]).then_inc(norm_dve, 1)
            else:
                dve.wait_ge(norm_dve, before)
                nc.vector.tensor_tensor(SS[:, 0:width], SS[:, 0:width], TMP[:, slot, 0:width],
                                        ALU.add).then_inc(norm_dve, 1)

        def act_squares(act, k, src, width):
            for kt in range(KT):
                act_square(act, 9 * k + kt - 1 if kt >= 2 else None, KT * k + kt, src[:, kt, :], kt % 2, width)

        def dve_sums(dve, k, width):
            for kt in range(KT):
                dve_sum(dve, KT * k + kt, kt == 0, kt % 2, width, 9 * k + kt)

        def pe_norm(pe, k, width, groups):
            pe.wait_ge(norm_dve, 9 * k + 8)
            last_col = [] if width == MEM else [(8, N - 128)]
            for c, first in [(c, 128 * c) for c in range(min(width, T) // 128)] + last_col:
                last = pe.matmul(ps[:, 6, c:c + 1], SS[:, first:first + 128], ONES[:, 0:1], start=True, stop=True)
            last.then_inc(norm_pe, 1)
            evacuated(pe, groups)
            pe.wait_ge(norm_dve, 9 * k + 9)
            for t in range(-(-width // TG)):
                c = slice(t * TG, min((t + 1) * TG, width))
                last = pe.matmul(ps[:, t, 0:c.stop - c.start], ONES, SS[:, c], start=True, stop=True)
            last.then_inc(norm_pe, 1)

        def act_norm(act, k, ks, width, hi=None):
            cols = 2 if width == MEM else 9
            act.wait_ge(norm_pe, 2 * k + 1)
            nc.scalar.activation(NRM[:, 0:cols], ps[:, 6, 0:cols], ACT.Sqrt, bias=EPSC,
                                 scale=1.0 / D).then_inc(norm_act, 1)
            act.wait_ge(norm_pe, 2 * k + 2)
            o, p = (t3(RB[:, :]), acc(0)) if width == N else (RB[:, 0:width], ps[:, 0, 0:width])
            nc.scalar.activation(o, p, ACT.Copy).then_inc(norm_act, 1)
            if hi is not None:
                act_round(act, k, hi, width)

        def act_round(act, k, hi, width):
            for kt in range(KT):
                act.wait_ge(xn_ready, KT * k + kt + 1)
                nc.scalar.activation(hi[:, kt, :], TMP[:, kt % 2, 0:width], ACT.Copy).then_inc(xh_ready, 1)

        def dve_norm_diag(dve, st, k, width):
            cols = 2 if width == MEM else 9
            dve.wait_ge(norm_act, 2 * k + 1)
            st.link(nc.vector.reciprocal(NRM[:, 0:cols], NRM[:, 0:cols]))
            if width == N:
                st.link(nc.vector.tensor_scalar(SS[:, T:N], IDENT[:, 120:128], NRM[:, 8:9], None, ALU.mult))
            c = min(width, T) // 128
            nc.vector.tensor_tensor(SS[:, 0:c * 128].rearrange("p (c i) -> p c i", i=128),
                                    IDENT.unsqueeze(1).to_broadcast([128, c, 128]),
                                    NRM[:, 0:c].unsqueeze(2).to_broadcast([128, c, 128]), ALU.mult).then_inc(norm_dve, 1)
            dve.wait_ge(norm_act, 2 * k + 2)

        def dve_norm(dve, st, kn, k, src, g, width, hi, lo):
            dve_norm_diag(dve, st, kn, width)
            for kt in range(KT + 1):
                if kt < KT:
                    nc.vector.scalar_tensor_tensor(out=TMP[:, kt % 2, 0:width], in0=src[:, kt, :],
                                                   scalar=GAIN[:, g, kt:kt + 1], in1=RB[:, 0:width],
                                                   op0=ALU.mult, op1=ALU.mult).then_inc(xn_ready, 1)
                if kt >= 1:
                    dve_rest(dve, k, kt - 1, width, hi, lo)

        def dve_rest(dve, k, kt, width, hi, lo):
            dve.wait_ge(xh_ready, KT * k + kt + 1)
            nc.vector.tensor_tensor(lo[:, kt, :], TMP[:, kt % 2, 0:width], hi[:, kt, :].bitcast(F32),
                                    ALU.subtract).then_inc(xl_ready, 1)
            dve.wait_ge(xl_ready, KT * k + kt + 1)

        MEMT = at("MEMT", [128, KT, MEM], O_XL)
        MEMH = at("MEMH", [128, KT, MEM], O_XL + 4 * 2048, F32R)
        MEML = at("MEML", [128, KT, MEM], O_XL + 4 * 4096, F32R)
        LVLIN = at("LVLIN", [128, LEVELS, 128], O_XL + 4 * 6144)
        MEMK = area("MEMK", [128, KT, MEM], 0)
        MEMV = area("MEMV", [128, 2, D], 2048)
        XIN = area("XIN", [128, KT, N], ARENA - KT * N)
        mem_in, x_in, mem_kv_out = sem("mem_in"), sem("x_in"), sem("mem_kv_out")

        def pool_load_first(pool):
            pool.dma_start(MEMT[:], I["memT"]).then_inc(mem_in, 16)
            for dst, name in ((CF, "cf"), (LVLIN, "lvl"), (SC, "sc"), (WALPHA, "walpha")):
                pool.dma_start(dst[:], I[name]).then_inc(consts_in, 16)
            for dst, name in ((SPAR, "s5par"), (SB, "s5b"), (SCC, "s5c"), (H0, "s5h0")):
                pool.dma_start(dst[:], I[name]).then_inc(s5_in, 16)
            pool.dma_start(XIN[:], I["xT"]).then_inc(x_in, 16)

        def pool_store_mem(pool):
            evacuated(pool, 16)
            pool.dma_start(O["mem_k"], MEMK[:]).then_inc(mem_kv_out, 16)
            pool.dma_start(O["mem_v"], MEMV[:]).then_inc(mem_kv_out, 16)

        def act_mem(act):
            act.wait_ge(mem_in, 16)
            act_squares(act, 0, MEMT, MEM)
            act_hi(act, 0, 0, 16, None)
            act_hi(act, 1, 1, 16, None)
            act.wait_ge(consts_in, 64)
            act.wait_ge(s5_in, 64)
            nc.scalar.activation(W(0), SPAR[:, 2, :], ACT.Exp).then_inc(s5_exp, 1)
            act_norm(act, 0, 0, MEM, MEMH)
            act.wait_ge(s5_red, 1)
            nc.scalar.activation(W(1), W(4), ACT.Exp).then_inc(s5_exp, 1)
            nc.scalar.activation(W(2), W(5), ACT.Sin).then_inc(s5_sin, 1)
            nc.scalar.activation(W(3), W(5), ACT.Sin, scale=0.5).then_inc(s5_sin, 1)
            with act.Fori(0, 4) as i:
                for s in range(2):
                    act.wait_ge(acc_ready, i * 2 + (s + 1))
                    nc.scalar.activation(MEMK[:, bass.ds(i * 2 + s, 1), :].rearrange("p a m -> p (a m)"),
                                         ps[:, 3 * s, 0:MEM], ACT.Copy).then_inc(acc_free[s], 1)
                    act_hi(act, None, s, i * 16 + 32, None)
            act.wait_ge(x_in, 16)
            act.wait_ge(xl_ready, KT)
            with act.Fori(0, 4) as i:
                for s in range(2):
                    act.wait_ge(acc_ready, i * 2 + (s + 9))
                    nc.scalar.activation(MEMV[:, :, bass.ts(i * 2 + s, 128)],
                                         ps[:, 3 * s:3 * s + 2, 0:128], ACT.Copy).then_inc(acc_free[s], 1)
                    act_hi(act, None, s, i * 16 + 96, None)
                    act_square(act, i * 2 + (8 + s), None, XIN[:, bass.ds(i * 2 + s, 1), :].rearrange("p a n -> p (a n)"), s, N)

        def dve_mem(dve, st):
            dve.wait_ge(mem_in, 16)
            dve_sums(dve, 0, MEM)
            dve.wait_ge(consts_in, 64)
            dve_lo(dve, 0, 0)
            dve_lo(dve, 1, 1)
            dve_norm(dve, st, 0, 0, MEMT, 1, MEM, MEMH, MEML)
            dve_project(dve, SL_CK, 8)
            dve.wait_ge(s5_den, 1)
            nc.vector.reciprocal(W(14), W(11)).then_inc(s5_rec, 1)
            st.link(nc.vector.tensor_copy(LVL[:], LVLIN[:]))
            st.link(nc.vector.memset(SS[:, :], 0.0))
            with dve.Fori(0, 4) as i:
                for s in range(2):
                    dve_lo(dve, i * 2 + (SL_CV + s + 2), s)
                    dve_sum(dve, i * 2 + (8 + s), False, s, N, i * 2 + (9 + s))

        def pe_mem(pe):
            pe.wait_ge(consts_in, 64)
            pe_norm(pe, 0, MEM, 0)
            pe.wait_ge(xl_ready, KT)

            def keys(n, s):
                pe.wait_ge(w_lo, n + 1)
                split_product(pe, [ps[:, 3 * s, 0:MEM]], s, lambda k, t: MEMH[:, k, :],
                              lambda k, t: MEML[:, k, :], 0, KT).then_inc(acc_ready, 1)

            keys(0, 0)
            keys(1, 1)
            with pe.Fori(0, 3) as i:
                for s in range(2):
                    pe.wait_ge(acc_free[s], i + 1)
                    keys(i * 2 + (s + 2), s)
            with pe.Fori(0, 4) as i:
                for s in range(2):
                    pe.wait_ge(w_lo, i * 2 + (s + 9))
                    pe.wait_ge(acc_free[s], i + 4)
                    for k in range(KT):
                        for mt in range(2):
                            out = ps[:, 3 * s + mt, 0:128]
                            c = slice(mt * 128, mt * 128 + 128)
                            pe.matmul(out, MEMH[:, k, c], WH[:, s, k, :], start=(k == 0), stop=False)
                            pe.matmul(out, MEMH[:, k, c], WL[:, s, k, :], start=False, stop=False)
                            last = pe.matmul(out, MEML[:, k, c], WH[:, s, k, :], start=False,
                                             stop=(k == KT - 1))
                    last.then_inc(acc_ready, 1)

        SU = area("SU", [128, 4 * N], 0)
        SUT = SU[:, :].rearrange("p (q n) -> p q n", n=N)

        def act_mix_in(act):
            act_norm(act, 1, 1, N, XH)
            act_project(act, SL_SPECIAL, G_SPECIAL, 1, GT, 0)
            act.wait_ge(mem_kv_out, 32)
            act_project(act, SL_SU, G_SU, 4, SU, 0)

        def dve_mix_in(dve, st):
            dve_norm(dve, st, 1, 1, XIN, 0, N, XH, XL)
            dve_project(dve, SL_SPECIAL, 1)
            dve_project(dve, SL_SU, 4)

        def pe_mix_in(pe):
            pe_norm(pe, 1, N, 16)
            pe_first(pe, SL_SPECIAL, G_SPECIAL, 1)
            pe_project(pe, SL_SU + 1, G_SU + 1, 3)

        pos = [4 * N]

        def nxt(name, shape):
            t = area(name, shape, pos[0])
            pos[0] += (math.prod(shape[1:]) + 7) // 8 * 8
            return t

        SPAR = nxt("SPAR", [128, 3, 32])
        USS = at("USS", [8, 8, 8, 16], O_ARENA + 4 * pos[0])
        SB, SCC = nxt("SB", [128, 2, 32, 16]), nxt("SCC", [128, 2, 32, 16])
        H0 = nxt("H0", [128, 2, 32, 8])
        BB, IBB = nxt("BB", [128, 32, 16]), nxt("IBB", [128, 32, 16])
        PW, PWD = nxt("PW", [128, 2, 32, 9]), nxt("PWD", [128, 2, 32, 8])
        WP = nxt("WP", [128, 15, 32])
        XP = nxt("XP", [128, 8, 8, 16])
        RC = (nxt("RC0", [128, 8, 128]), at("RC1", [128, 8, 128], O_RB))
        RS = (nxt("RS0", [128, 8, 128]), at("RS1", [128, 8, 128], O_ROWS))
        OT = (nxt("OT0", [128, 8, 9, 16]), nxt("OT1", [128, 8, 9, 16]))
        assert pos[0] - 1152 <= ARENA - KT * N
        USU, U = nxt("USU", [128, 8, 128]), nxt("U", [128, 8, 128])
        UG = USU[:, :, :].rearrange("p g (j c) -> p g j c", c=16)
        EP = USU
        BT1, BT2 = nxt("BT1", [128, 8, 128]), nxt("BT2", [128, 8, 128])
        TT, HST = nxt("TT", [128, 8, 128]), nxt("HST", [128, 8, 129])
        GK = nxt("GK", [128, 128])
        US, HN = nxt("US", [128, 8, 8]), nxt("HN", [128, 8, 8])
        SOUT, USS2 = nxt("SOUT", [128, 32, 9]), nxt("USS2", [8, 128])
        W32 = at("W32", [128, 32, 32], O_ROWS)
        SCR = at("SCR", [128, 1024], O_WPL)
        T4 = at("T4", [128, 2, 8, 128], O_TMP)
        s5_gk = sem("s5_gk")
        s5_den, s5_rec, pool_step = sem("s5_den"), sem("s5_rec"), sem("pool_step")
        s5_in, s5_exp, s5_red, s5_sin = sem("s5_in"), sem("s5_exp"), sem("s5_red"), sem("s5_sin")
        s5_tables = sem("s5_tables")
        s5_tok_out, s5_u_out, s5_bt_out, s5_tt_out = sem("s5_tok_out"), sem("s5_u_out"), sem("s5_bt_out"), sem("s5_tt_out")
        s5_scan, s5_h, s5_y_out, s5_done = sem("s5_scan"), sem("s5_h"), sem("s5_y_out"), sem("s5_done")
        s5_st_out, s5_su_out, s5_hn, s5_ys_out = sem("s5_st_out"), sem("s5_su_out"), sem("s5_hn"), sem("s5_ys_out")
        s5_pe = sem("s5_pe")
        s5_at = counts("tok", "bt", "gk", "u", "tt", "s", "swap", "st", "su", "ss", "y", "yt", "ys", "yst")
        s5_stored = sem("s5_stored")
        W = lambda k: W32[:, k, :] if k < 17 else WP[:, k - 17, :]

        def pool_s5_prepare(pool, st):
            L = st.link
            tt = lambda o_, a, b_, op: L(nc.gpsimd.tensor_tensor(o_, a, b_, op))
            M, AD, SU_ = ALU.mult, ALU.add, ALU.subtract
            pool.wait_ge(s5_in, 64)
            pool.wait_ge(s5_exp, 1)
            tt(W(4), SPAR[:, 0, :], W(0), M)
            tt(W(6), SPAR[:, 1, :], W(0), M)
            L(nc.gpsimd.tensor_scalar(W(7), W(6), 1.0 / (2 * math.pi), 12582912.0, M, AD))
            L(nc.gpsimd.tensor_scalar(W(7), W(7), 12582912.0, None, SU_))
            c1 = 6.28125
            c2 = float(np.float32(2 * math.pi - c1).view(np.uint32) & 0xFFFFF000)
            c2 = float(np.array([int(c2)], np.uint32).view(np.float32)[0])
            c3 = float(2 * math.pi - c1 - c2)
            for c in (c1, c2, c3):
                L(nc.gpsimd.tensor_scalar(W(8), W(7), -c, None, M))
                tt(W(6), W(6), W(8), AD)
            nc.gpsimd.tensor_scalar(W(5), W(6), 3.1415925, -3.1415925, ALU.min, ALU.max).then_inc(s5_red, 1)
            pool.wait_ge(s5_red, 1)
            pool.wait_ge(s5_sin, 2)
            pool.wait_ge(s5_exp, 2)
            tt(W(10), W(3), W(3), M)
            L(nc.gpsimd.tensor_scalar(W(10), W(10), -2.0, 1.0, M, AD))
            tt(PW[:, 0, :, 1], W(1), W(10), M)
            tt(PW[:, 1, :, 1], W(1), W(2), M)
            L(nc.gpsimd.memset(PW[:, 0, :, 0:1], 1.0))
            L(nc.gpsimd.memset(PW[:, 1, :, 0:1], 0.0))
            ar, ai = PW[:, 0, :, 1], PW[:, 1, :, 1]
            for k in range(2, 9):
                tt(W(11), PW[:, 0, :, k - 1], ar, M)
                tt(W(12), PW[:, 1, :, k - 1], ai, M)
                tt(PW[:, 0, :, k], W(11), W(12), SU_)
                tt(W(11), PW[:, 0, :, k - 1], ai, M)
                tt(W(12), PW[:, 1, :, k - 1], ar, M)
                tt(PW[:, 1, :, k], W(11), W(12), AD)
            for k in range(8):
                L(nc.gpsimd.tensor_copy(PWD[:, :, :, k], PW[:, :, :, 7 - k]))
            lr, li = SPAR[:, 0, :], SPAR[:, 1, :]
            L(nc.gpsimd.tensor_scalar(W(13), ar, -1.0, None, AD))
            tt(W(11), lr, lr, M)
            tt(W(12), li, li, M)
            nc.gpsimd.tensor_tensor(W(11), W(11), W(12), AD).then_inc(s5_den, 1)
            pool.wait_ge(s5_rec, 1)
            tt(W(11), W(13), lr, M)
            tt(W(12), ai, li, M)
            tt(W(11), W(11), W(12), AD)
            tt(W(15), W(11), W(14), M)
            tt(W(11), ai, lr, M)
            tt(W(12), W(13), li, M)
            tt(W(11), W(11), W(12), SU_)
            tt(W(16), W(11), W(14), M)
            L(nc.gpsimd.tensor_scalar(SB[:, 1], SB[:, 1], NSGN, None, M))
            L(nc.gpsimd.tensor_scalar(SCC[:, 0], SCC[:, 0], SGN, None, M))
            L(nc.gpsimd.tensor_scalar(H0[:, 1], H0[:, 1], NSGN, None, M))
            fr = W(15).unsqueeze(2).to_broadcast([128, 32, 16])
            fi = W(16).unsqueeze(2).to_broadcast([128, 32, 16])
            t5 = SCR[:, 0:512].rearrange("p (g c) -> p g c", c=16)
            tt(BB[:, :, :], SB[:, 0], fr, M)
            tt(t5, SB[:, 1], fi, M)
            tt(BB[:, :, :], BB[:, :, :], t5, AD)
            tt(IBB[:, :, :], SB[:, 1], fr, M)
            tt(t5, SB[:, 0], fi, M)
            tt(IBB[:, :, :], IBB[:, :, :], t5, SU_)
            L(nc.gpsimd.memset(USS[:, :, :, :], 0.0))
            tt(W(17), W(1), W(1), M)
            tt(W(17), W(17), W(17), M)
            tt(W(17), W(17), W(17), M)
            cr, ci = W(10), W(2)
            for k in range(9):
                at_ = (8, 4)[k] if k < 2 else 18 + 2 * (k - 2)
                nr, ni = W(at_), W(at_ + 1)
                tt(W(11), cr, cr, M)
                tt(W(12), ci, ci, M)
                tt(W(13), cr, ci, M)
                tt(nr, W(11), W(12), SU_)
                L(nc.gpsimd.tensor_scalar(ni, W(13), 2.0, None, M))
                cr, ci = nr, ni

        def pool_s5_tables(pool, st, q):
            tt = lambda o_, a, b_, op: st.link(nc.gpsimd.tensor_tensor(o_, a, b_, op))
            M, AD, SU_ = ALU.mult, ALU.add, ALU.subtract
            gs = slice(8 * q, 8 * q + 8)
            rc, rs, ot = RC[q % 2], RS[q % 2], OT[q % 2]
            if q >= 2:
                pool.wait_ge(s5_h, q - 1)
            st.link(nc.gpsimd.memset(rc[:, :, 0:1], 1.0))
            st.link(nc.gpsimd.memset(rs[:, :, 0:1], 0.0))
            for k in range(7):
                w = 1 << k
                ur = W(18 + 2 * k)[:, gs].unsqueeze(2).to_broadcast([128, 8, w])
                ui = W(19 + 2 * k)[:, gs].unsqueeze(2).to_broadcast([128, 8, w])
                a0, a1 = (SCR[:, 512 * x:512 * x + 8 * w].rearrange("p (g n) -> p g n", n=w) for x in range(2))
                tt(a0, rc[:, :, 0:w], ur, M)
                tt(a1, rs[:, :, 0:w], ui, M)
                tt(rc[:, :, w:2 * w], a0, a1, SU_)
                tt(a0, rc[:, :, 0:w], ui, M)
                tt(a1, rs[:, :, 0:w], ur, M)
                tt(rs[:, :, w:2 * w], a0, a1, AD)
            if q >= 2:
                pool.wait_ge(s5_pe, s5_at("yst", q - 1))
            for half in range(2):
                g4, o4 = slice(8 * q + 4 * half, 8 * q + 4 * half + 4), slice(4 * half, 4 * half + 4)
                sh9 = [128, 4, 9, 16]
                t9 = SCR[:, 0:576].rearrange("p (g t c) -> p g t c", t=9, c=16)
                tt(ot[:, o4, :, :], SCC[:, 0, g4, :].unsqueeze(2).to_broadcast(sh9),
                   PW[:, 0, g4, :].unsqueeze(3).to_broadcast(sh9), M)
                tt(t9, SCC[:, 1, g4, :].unsqueeze(2).to_broadcast(sh9),
                   PW[:, 1, g4, :].unsqueeze(3).to_broadcast(sh9), M)
                tt(ot[:, o4, :, :], ot[:, o4, :, :], t9, SU_)
            if q:
                pool.wait_ge(s5_pe, s5_at("gk", q))
            sh = [128, 8, 8, 16]
            t6 = SCR[:, :].rearrange("p (g j c) -> p g j c", j=8, c=16)
            tt(XP[:, :, :, :], BB[:, gs, :].unsqueeze(2).to_broadcast(sh), PWD[:, 0, gs, :].unsqueeze(3).to_broadcast(sh), M)
            tt(t6, IBB[:, gs, :].unsqueeze(2).to_broadcast(sh), PWD[:, 1, gs, :].unsqueeze(3).to_broadcast(sh), M)
            nc.gpsimd.tensor_tensor(XP[:, :, :, :], XP[:, :, :, :], t6, AD).then_inc(s5_tables, 1)
            pool.wait_ge(s5_tables, q + 1)

        def pool_s5(pool, st):
            pool.wait_ge(xl_ready, 2 * KT)
            for q in range(1, 4):
                pool_s5_tables(pool, st, q)
            pool.wait_ge(s5_done, 4)
            pool.dma_start(O["s5_state"], SOUT[:]).then_inc(s5_stored, 16)

        def act_s5(act):
            for q in range(4):
                act.wait_ge(s5_pe, s5_at("tok", q + 1))
                if q:
                    act.wait_ge(s5_pe, s5_at("yt", q))
                for k in range(2):
                    nc.scalar.activation(UG[:, :, 4 * k:4 * k + 4, :].rearrange("p g j c -> p j g c"),
                                         ps[:, k, :].rearrange("p (j g c) -> p j g c", j=4, c=16),
                                         ACT.Copy).then_inc(s5_tok_out, 1)
                act.wait_ge(s5_pe, s5_at("gk", q + 1))
                nc.scalar.activation(GK[:, :], ps[:, 6, 0:128], ACT.Copy).then_inc(s5_gk, 1)
                act.wait_ge(s5_pe, s5_at("u", q + 1))
                if q:
                    act.wait_ge(s5_pe, s5_at("y", q))
                nc.scalar.activation(U[:, :, :].rearrange("p j f -> p (j f)").rearrange("p (a b) -> p a b", b=512),
                                     ps[:, 2:4, :], ACT.Copy).then_inc(s5_u_out, 1)
                act.wait_ge(s5_pe, s5_at("bt", q + 1))
                if q:
                    act.wait_ge(s5_pe, s5_at("ss", q))
                nc.scalar.activation(BT1[:, :, :].rearrange("p j f -> p (j f)").rearrange("p (a b) -> p a b", b=512),
                                     ps[:, 4:6, :], ACT.Copy).then_inc(s5_bt_out, 1)
                nc.scalar.activation(BT2[:, :, 0:64], two(4)[:, :, 64:128], ACT.Copy, scale=-1.0).then_inc(s5_bt_out, 1)
                nc.scalar.activation(BT2[:, :, 64:128], two(4)[:, :, 0:64], ACT.Copy).then_inc(s5_bt_out, 1)
                act.wait_ge(s5_pe, s5_at("tt", q + 1))
                nc.scalar.activation(TT[:, :, :].rearrange("p g (t c) -> p t g c", c=16),
                                     two(0).rearrange("p t (g c) -> p t g c", c=16), ACT.Copy).then_inc(s5_tt_out, 1)
                act.wait_ge(s5_pe, s5_at("st", q + 1))
                if q:
                    act.wait_ge(s5_pe, s5_at("su", q))
                nc.scalar.activation(USS[:, :, 7, :], ps[0:8, 4, 0:128].rearrange("p (g c) -> p g c", c=16), ACT.Copy).then_inc(s5_st_out, 1)
                act.wait_ge(s5_pe, s5_at("su", q + 1))
                nc.scalar.activation(US[:, :, :].rearrange("p g b -> p (g b)"), ps[:, 5, 0:64],
                                     ACT.Copy).then_inc(s5_su_out, 1)
                act.wait_ge(s5_pe, s5_at("y", q + 1))
                for h in range(2):
                    nc.scalar.activation(
                        USU[:, :, h * 64:h * 64 + 64].rearrange("p t (g c) -> p g t c", c=16),
                        ps[:, h, :].rearrange("p (g t c) -> p g t c", g=4, c=16), ACT.Copy).then_inc(s5_y_out, 1)
                act.wait_ge(s5_pe, s5_at("ys", q + 1))
                nc.scalar.activation(USS2[:, :], ps[0:8, 7, 0:128], ACT.Copy).then_inc(s5_ys_out, 1)

        def dve_s5(dve, st):
            L = st.link
            tt = lambda o_, a, b_, op: L(nc.vector.tensor_tensor(o_, a, b_, op))
            M, AD, SU_ = ALU.mult, ALU.add, ALU.subtract
            L(nc.vector.memset(HST[:, :, 0:1], 0.0))
            for q in range(4):
                gs = slice(8 * q, 8 * q + 8)
                rc, rs = RC[q % 2], RS[q % 2]
                dve.wait_ge(s5_tables, q + 1)
                dve.wait_ge(s5_pe, s5_at("s", q + 1))
                b2 = lambda k: ps[:, k:k + 2, :].rearrange("p a (g n) -> p a g n", n=128)
                r4 = lambda x: x.rearrange("p (a g) n -> p a g n", a=2)
                tt(r4(T4[:, 0]), b2(2), r4(rc[:, :, :]), M)
                tt(r4(T4[:, 1]), b2(4), r4(rs[:, :, :]), M)
                tt(T4[:, 0], T4[:, 0], T4[:, 1], SU_)
                for g in range(8):
                    sc = nc.vector.tensor_tensor_scan(EP[:, g, :], W(17)[:, 8 * q + g:8 * q + g + 1].to_broadcast([128, 128]),
                                                      T4[:, 0, g, :], 0.0, ALU.mult, ALU.add)
                    sc.then_inc(s5_scan, 1)
                dve.wait_ge(s5_scan, 8 * q + 8)
                tt(T4[:, 0], EP[:, :, :], rc[:, :, :], M)
                dve.wait_ge(s5_pe, s5_at("swap", q + 1))
                tt(r4(T4[:, 1]), b2(6), r4(rs[:, :, :]), M)
                if q:
                    dve.wait_ge(s5_pe, s5_at("y", q))
                nc.vector.tensor_tensor(HST[:, :, 1:129], T4[:, 0], T4[:, 1], AD).then_inc(s5_h, 1)
                dve.wait_ge(s5_h, q + 1)
                L(nc.vector.tensor_copy(SOUT[:, gs, 0], HST[:, :, 128]))
                dve.wait_ge(s5_pe, s5_at("ss", q + 1))
                sh8 = [128, 8, 8]
                h0, ih0 = H0[:, 0, gs, :], H0[:, 1, gs, :]
                a_r = PW[:, 0, gs, 1:2].to_broadcast(sh8)
                a_i = PW[:, 1, gs, 1:2].to_broadcast(sh8)
                t8, t8b = T4[:, 0, 0, 0:64].rearrange("p (g b) -> p g b", b=8), T4[:, 1, 0, 0:64].rearrange("p (g b) -> p g b", b=8)
                tt(t8, h0, a_r, M)
                tt(t8b, ih0, a_i, M)
                tt(t8, t8, t8b, AD)
                nc.vector.tensor_tensor(HN[:, :, :], t8, ps[:, 6, 0:64].rearrange("p (g b) -> p g b", b=8), AD).then_inc(s5_hn, 1)
                dve.wait_ge(s5_hn, q + 1)
                L(nc.vector.tensor_copy(SOUT[:, gs, 1:9], HN[:, :, :]))
                dve.wait_ge(s5_pe, s5_at("yt", q + 1))
                for k in range(2):
                    v = SUT[:, q, 0:T].rearrange("p (n t) -> p t n", t=8)[:, 4 * k:4 * k + 4, :]
                    L(nc.vector.scalar_tensor_tensor(out=v, in0=v, scalar=S5D[:, q:q + 1],
                                                     in1=ps[:, 2 + k, :].rearrange("p (t n) -> p t n", n=128),
                                                     op0=M, op1=AD))
                dve.wait_ge(s5_pe, s5_at("yst", q + 1))
                v = SUT[:, q, T:N]
                nc.vector.scalar_tensor_tensor(out=v, in0=v, scalar=S5D[:, q:q + 1], in1=ps[:, 7, 128:136],
                                               op0=M, op1=AD).then_inc(s5_done, 1)

        def pe_s5(pe):
            evacuated(pe, G_SU + 4)
            for q in range(4):
                su = SUT[:, q, 0:T].rearrange("p (n j) -> p j n", j=8)
                for j in range(8):
                    last = pe.transpose(ps[:, j // 4, (j % 4) * 128:(j % 4) * 128 + 128], su[:, j, :], IDENT)
                last.then_inc(s5_pe, 1)
                pe.wait_ge(s5_tables, q + 1)
                for g in range(8):
                    last = pe.transpose(ps[:, 4 + g // 4, (g % 4) * 128:(g % 4) * 128 + 128],
                                        XP[:, g, :, :].rearrange("p j c -> p (j c)"), IDENT)
                last.then_inc(s5_pe, 1)
                for g in range(8):
                    last = pe.matmul(ps[:, 6, 16 * g:16 * g + 16], XP[:, g, :, :].rearrange("p j c -> p (j c)"),
                                     OT[q % 2][:, g, 0, :], start=True, stop=True)
                last.then_inc(s5_pe, 1)
                pe.wait_ge(s5_tok_out, 2 * q + 2)
                if q:
                    pe.wait_ge(s5_done, q)
                for g in range(8):
                    last = pe.transpose(ps[:, 2 + g // 4, (g % 4) * 128:(g % 4) * 128 + 128],
                                        USU[:, g, :], IDENT)
                last.then_inc(s5_pe, 1)
                pe.wait_ge(s5_gk, q + 1)
                for t in range(8):
                    last = pe.matmul(two(0)[:, t, :], SHIFT[:, 16 * (7 - t):16 * (7 - t) + 128], GK[:, :],
                                     start=True, stop=True)
                last.then_inc(s5_pe, 1)
                pe.wait_ge(s5_u_out, q + 1)
                pe.wait_ge(s5_bt_out, 3 * q + 3)
                for g in range(8):
                    c = slice((g % 4) * 128, (g % 4) * 128 + 128)
                    pe.matmul(ps[:, 2 + g // 4, c], BT1[:, g, :], U[:, g, :], start=True, stop=True)
                    last = pe.matmul(ps[:, 4 + g // 4, c], BT2[:, g, :], U[:, g, :], start=True, stop=True)
                last.then_inc(s5_pe, 1)
                pe.wait_ge(s5_scan, 8 * q + 8)
                for k in range(2):
                    last = pe.matmul(ps[:, 6 + k, :], PSW, EP[:, 4 * k:4 * k + 4, :].rearrange("p g n -> p (g n)"),
                                     start=True, stop=True)
                last.then_inc(s5_pe, 1)
                pe.transpose(ps[0:8, 4, 0:128], SUT[:, q, T:N], IDENT).then_inc(s5_pe, 1)
                pe.wait_ge(s5_st_out, q + 1)
                for g in range(8):
                    last = pe.transpose(ps[:, 5, g * 8:g * 8 + 8], USS[:, g, :, :].rearrange("p j c -> p (j c)"), IDENT[0:8, 0:8])
                last.then_inc(s5_pe, 1)
                pe.wait_ge(s5_h, q + 1)
                pe.wait_ge(s5_su_out, q + 1)
                for g in range(8):
                    last = pe.matmul(ps[:, 6, g * 8:g * 8 + 8], BT1[:, g, :], US[:, g, :], start=True, stop=True)
                last.then_inc(s5_pe, 1)
                pe.wait_ge(s5_tt_out, q + 1)
                for g in range(8):
                    c = slice((g % 4) * 128, (g % 4) * 128 + 128)
                    pe.matmul(ps[:, g // 4, c], U[:, g, :], TT[:, g, :], start=True, stop=False)
                    last = pe.matmul(ps[:, g // 4, c], HST[:, g, 0:128],
                                     OT[q % 2][:, g, 1:9, :].rearrange("p t c -> p (t c)"), start=False, stop=True)
                last.then_inc(s5_pe, 1)
                pe.wait_ge(s5_y_out, 2 * q + 2)
                for t in range(8):
                    last = pe.transpose(ps[:, 2 + t // 4, (t % 4) * 128:(t % 4) * 128 + 128], USU[:, t, :], IDENT)
                last.then_inc(s5_pe, 1)
                pe.wait_ge(s5_hn, q + 1)
                for g in range(8):
                    last = pe.matmul(ps[0:8, 7, g * 16:g * 16 + 16], HN[:, g, :], OT[q % 2][:, g, 0, :],
                                     start=True, stop=True)
                last.then_inc(s5_pe, 1)
                pe.wait_ge(s5_ys_out, q + 1)
                pe.transpose(ps[:, 7, 128:136], USS2[:, :], IDENT[0:8, 0:8]).then_inc(s5_pe, 1)

        YC = area("YC", [128, 4, N], 8256)
        glu_in, glu_sig, glu_out, yc_stored = sem("glu_in"), sem("glu_sig"), sem("glu_out"), sem("yc_stored")

        def plain_product(pe, n, g, slot, gslot, rhs):
            pe.wait_ge(wp_loaded[slot], n)
            pe.wait_ge(acc_free[gslot], g // 2)
            for k in range(4):
                for t in range(NTG):
                    last = pe.matmul(banks(gslot)[t], WPL[:, slot, k, :], rhs(k, t), start=(k == 0), stop=(k == 3))
            last.then_inc(acc_ready, 1)

        def pe_glu(pe):
            pe.wait_ge(glu_in, 4)
            for m in range(4):
                plain_product(pe, 16 * (m // 2 + 1), GR_GLU + m, m % 2, (GR_GLU + m) % 2,
                              lambda k, t: SUT[:, k, t * TG:(t + 1) * TG])

        def act_glu(act):
            act.wait_ge(s5_done, 4)
            for q in range(4):
                nc.scalar.activation(SUT[:, q, :], SUT[:, q, :], ACT.Gelu_apprx_tanh).then_inc(glu_in, 1)
            for m in range(4):
                act.wait_ge(acc_ready, GR_GLU + m + 1)
                if m >= 2:
                    act.wait_ge(glu_out, m - 1)
                nc.scalar.activation(t3(TMP[:, m % 2, :]), acc((GR_GLU + m) % 2), ACT.Sigmoid).then_inc(glu_sig, 1)

        def dve_glu(dve):
            for m in range(4):
                dve.wait_ge(glu_sig, m + 1)
                dve.sem_inc(acc_free[(GR_GLU + m) % 2], 1)
                nc.vector.tensor_tensor(YC[:, m, :], SUT[:, m, :], TMP[:, m % 2, :], ALU.mult).then_inc(glu_out, 1)

        def pool_glu(pool):
            for m in range(4):
                if m >= 2:
                    pool.wait_ge(acc_ready, GR_GLU + m - 1)
                pool.dma_start(WPL[:, m % 2], I["wplain"][m]).then_inc(wp_loaded[m % 2], 16)

        def pool_store_yc(pool):
            pool.wait_ge(glu_out, 4)
            pool.dma_start(I["yc"], YC[:]).then_inc(yc_stored, 16)

        hn_sq, hn_sum, hn_rms, hn_done = sem("hn_sq"), sem("hn_sum"), sem("hn_rms"), sem("hn_done")

        def act_headnorm(act, k, tiles):
            nc.scalar.activation(TMP[:, 0, 0:4 * B].rearrange("p (h b) -> p h b", b=B), tiles[:, :, T:N],
                                 ACT.Square).then_inc(hn_sq, 1)
            act.wait_ge(hn_sum, k + 1)
            nc.scalar.activation(RB[:, 0:4 * B], ps[:, 6, 0:4 * B], ACT.Sqrt, bias=EPSC, scale=1.0 / 128).then_inc(hn_rms, 1)

        def pe_headnorm(pe, k):
            pe.wait_ge(hn_sq, k + 1)
            pe.matmul(ps[:, 6, 0:4 * B], ONES, TMP[:, 0, 0:4 * B], start=True, stop=True).then_inc(hn_sum, 1)

        def dve_headnorm(dve, st, k, tiles, gain):
            dve.wait_ge(hn_rms, k + 1)
            st.link(nc.vector.reciprocal(RB[:, 0:4 * B], RB[:, 0:4 * B]))
            for h in range(4):
                o_ = tiles[:, h, T:N]
                nc.vector.scalar_tensor_tensor(out=o_, in0=o_, scalar=gain[:, h:h + 1], in1=RB[:, B * h:B * h + B],
                                               op0=ALU.mult, op1=ALU.mult).then_inc(hn_done, 1)
            dve.wait_ge(hn_done, 4 * k + 4)

        MQ = area("MQ", [128, 4 * N], 0)
        MK = area("MKV", [128, 8 * N], 4 * N)
        MQT = MQ[:, :].rearrange("p (h n) -> p h n", n=N)
        MKT = MK[:, 0:4 * N].rearrange("p (h n) -> p h n", n=N)
        MVT = MK[:, 4 * N:8 * N].rearrange("p (h n) -> p h n", n=N)
        pos[0] = 12 * N
        V1 = nxt("V1", [128, NCH, 256])
        KE = nxt("KE", [128, NCH, 128])
        ST = nxt("ST", [128, NCH, 128])
        QA = nxt("QA", [128, NCH, 128])
        CC = nxt("CC", [128, NCH + 1, 256])
        CS = nxt("CS", [128, B, 128])
        NS = nxt("NS", [128, 4, B])
        EB = nxt("EB", [128, 4, 8])
        BCOL = nxt("BCOL", [128, NCH, 4])
        ECOL, EMCOL = nxt("ECOL", [128, NCH, 4]), nxt("EMCOL", [128, NCH, 4])
        DEN = nxt("DEN", [128, 3, NCH])
        KS, QN, RS8 = nxt("KS", [128, B]), nxt("QN", [128, B]), nxt("RS8", [128, B])
        KST = nxt("KST", [8, 128])
        VD = nxt("VD", [8, 8, 128])
        MOUT = nxt("MOUT", [4, 9])
        M0 = nxt("M0", [4, 8])
        R = [at(f"R{k}", [4, N], O_ARENA + 4 * (12 * N + k * N)) for k in range(6)]
        R8 = [at(f"R8_{k}", [4, 8], O_ARENA + 4 * (18 * N + k * 8)) for k in range(6)]
        ml_in, ml_x, ml_l1 = sem("ml_in"), sem("ml_x"), sem("ml_l1")
        ml_e, ml_rows, ml_ej, ml_ecol = sem("ml_e"), sem("ml_rows"), sem("ml_ej"), sem("ml_ecol")
        ml_v, ml_exp, ml_ebo, ml_sq = sem("ml_v"), sem("ml_exp"), sem("ml_ebo"), sem("ml_sq")
        ml_cs_in, ml_rt, ml_on, ml_kst, ml_out = (sem("ml_cs_in"), sem("ml_rt"), sem("ml_on"), sem("ml_kst"), sem("ml_out"))
        ml_abs8, ml_gate, ml_y, yb_stored = sem("ml_abs8"), sem("ml_gate"), sem("ml_y"), sem("yb_stored")
        ml_pe, ml_dve = sem("ml_pe"), sem("ml_dve")
        ml_at = counts("tr", "ds", "ab", "eb", "dc", "nd", "st8", "kv", "ot", "os")
        ml_did = counts("ke", "st", "c", "ks", "div", "vd", "ms", "o", "cn", "qn")

        def spread(row):
            return IDENT[:, row:row + 1].to_broadcast([128, 128])

        def chunk(c):
            return slice(c * CH, (c + 1) * CH)

        def pool_mlstm(pool):
            pool.wait_ge(yc_stored, 16)
            pool.wait_ge(s5_stored, 16)
            pool.dma_start(M0[:, :], I["m0"]).then_inc(ml_in, 16)
            pool.dma_start(NS[:, :, :], I["n0"]).then_inc(ml_in, 16)
            for h in range(4):
                if h:
                    pool.wait_ge(ml_out, 32 * h)
                    pool.wait_ge(ml_pe, ml_at("os", h))
                pool.dma_start(CS[:, :, :], I["c0"][h]).then_inc(ml_cs_in, 16)
                pool.wait_ge(ml_dve, ml_did("cn", h + 1))
                pool.dma_start(O["c_s"][h], CS[:, :, :]).then_inc(ml_out, 16)
                pool.wait_ge(ml_dve, ml_did("c", h + 1))
                pool.dma_start(O["c_p"][h], CC[:, NCH, 0:129]).then_inc(ml_out, 16)
            pool.dma_start(O["n_s"], NS[:, :, :]).then_inc(ml_out, 16)
            pool.dma_start(O["m"], MOUT[:, :]).then_inc(ml_out, 16)

        def act_mlstm(act, st):
            act_project(act, SL_MQ, G_MQ, 4, MQ, 0, scale=128.0 ** -0.5)
            act.wait_ge(yc_stored, 16)
            act.wait_ge(ml_x, 1)
            st.link(nc.scalar.activation(R[3][:, :], R[3][:, :], ACT.Exp, scale=-1.0))
            nc.scalar.activation(R[3][:, :], R[3][:, :], ACT.Ln, bias=1.0).then_inc(ml_l1, 1)
            act_project(act, SL_MKV, G_MKV, 4, MK, 0)
            act.wait_ge(ml_e, 1)
            nc.scalar.activation(ROWS[64:68, 0:T], R[2][:, 0:T], ACT.Exp).then_inc(ml_rows, 1)
            nc.scalar.activation(R[4][:, 0:T], R[4][:, 0:T], ACT.Exp, scale=-1.0).then_inc(ml_rows, 1)
            nc.scalar.activation(R[5][:, 0:T], R[5][:, 0:T], ACT.Exp).then_inc(ml_rows, 1)
            nc.scalar.activation(ROWS[64:68, T:N], R8[1][:, :], ACT.Exp).then_inc(ml_rows, 1)
            nc.scalar.activation(ROWS[0:4, T:N], R8[3][:, :], ACT.Exp).then_inc(ml_rows, 1)
            nc.scalar.activation(ROWS[32:36, T:N], R8[4][:, :], ACT.Exp).then_inc(ml_rows, 1)
            nc.scalar.activation(ROWS[96:100, T:N], R8[2][:, :], ACT.Exp, scale=-1.0).then_inc(ml_rows, 1)
            act_project(act, SL_MKV + 4, G_MKV + 4, 4, MK, 4)
            for h in range(4):
                act.wait_ge(ml_pe, ml_at("tr", h + 1))
                if h:
                    act.wait_ge(ml_pe, ml_at("nd", h))
                else:
                    act.wait_ge(ml_ecol, 1)
                nc.scalar.activation(V1[:, :, 0:128], two(0), ACT.Copy).then_inc(ml_v, 1)
                act.wait_ge(ml_pe, ml_at("ds", h + 1))
                for c in range(NCH):
                    nc.scalar.activation(TMP[:, 0, chunk(c)], two(4)[:, c, :], ACT.Exp,
                                         bias=BCOL[:, c, h:h + 1]).then_inc(ml_exp, 1)
                act.wait_ge(ml_pe, ml_at("eb", h + 1))
                nc.scalar.activation(EB[:, :, :].rearrange("p a b -> p (a b)"), ps[:, 2, 0:32],
                                     ACT.Copy).then_inc(ml_ebo, 1)
                act.wait_ge(ml_pe, ml_at("st8", h + 1))
                nc.scalar.activation(KST[:, :], ps[0:8, 6, 0:128], ACT.Copy).then_inc(ml_kst, 1)
                act.wait_ge(ml_dve, ml_did("div", h + 1))
                nc.scalar.activation(TMP[:, 0, 0:T].rearrange("p (c i) -> p c i", i=128), KE[:, :, :],
                                     ACT.Square).then_inc(ml_sq, 1)
                act.wait_ge(ml_dve, ml_did("ms", h + 1))
                nc.scalar.activation(DEN[:, 2, :], DEN[:, 1, :], ACT.Sqrt, bias=EPSC, scale=1.0 / 128).then_inc(ml_rt, 1)
                act.wait_ge(ml_pe, ml_at("ot", h + 1))
                nc.scalar.activation(MQT[:, h, 0:T].rearrange("p (c i) -> p c i", i=128), two(0), ACT.Copy,
                                     scale=MLN[:, h:h + 1]).then_inc(ml_on, 1)
                act.wait_ge(ml_pe, ml_at("os", h + 1))
                nc.scalar.activation(RS8[:, :], ps[:, 5, 8:16], ACT.Abs).then_inc(ml_abs8, 1)

        def dve_mlstm(dve, st):
            L = st.link
            dve_project(dve, SL_MQ, 4)
            tt = lambda o_, a, b_, op: L(nc.vector.tensor_tensor(o_, a, b_, op))
            M, AD, SU_ = ALU.mult, ALU.add, ALU.subtract
            dve.wait_ge(ml_in, 32)
            L(nc.vector.memset(ROWS[:, :], 0.0))
            L(nc.vector.tensor_scalar(R[0][:, :], GT[32:36, :], BIF[32:36, :], None, AD))
            L(nc.vector.tensor_scalar(R[1][:, :], GT[64:68, :], BIF[64:68, :], None, AD))
            nc.vector.scalar_tensor_tensor(out=R[3][:, :], in0=R[1][:, :], scalar=-1.0, in1=R[1][:, :],
                                           op0=M, op1=ALU.max).then_inc(ml_x, 1)
            dve_project(dve, SL_MKV, 2)
            dve.wait_ge(ml_l1, 1)
            L(nc.vector.scalar_tensor_tensor(out=R[1][:, :], in0=R[1][:, :], scalar=0.0, in1=R[3][:, :],
                                             op0=ALU.min, op1=SU_))
            li, lf, b, m = R[0], R[1], R[3], R[4]
            for c in range(NCH):
                L(nc.vector.tensor_tensor_scan(b[:, chunk(c)], ONES[0:4, :], lf[:, chunk(c)], 0.0, M, AD))
            L(nc.vector.tensor_tensor_scan(m[:, 0:T], lf[:, 0:T], li[:, 0:T], 0.0, AD, ALU.max))
            dve_project(dve, SL_MKV + 2, 2)
            tt(ROWS[0:4, 0:T], b[:, 0:T], m[:, 0:T], SU_)
            tt(R[1][:, 0:T], li[:, 0:T], b[:, 0:T], SU_)
            c8 = lambda x: x.rearrange("p (c i) -> p c i", i=128)
            ends = lambda x: c8(x[:, 0:T])[:, :, 127]
            mp = R8[0]
            L(nc.vector.memset(mp[:, 0:1], 0.0))
            L(nc.vector.tensor_copy(mp[:, 1:8], ends(m)[:, 0:7]))
            tt(c8(R[2][:, 0:T]), c8(ROWS[0:4, 0:T]), mp[:, :].unsqueeze(2).to_broadcast([4, 8, 128]), AD)
            tt(R8[2][:, :], ends(b), ends(m), SU_)
            L(nc.vector.tensor_copy(R[5][:, 0:T], R[1][:, 0:T]))
            tt(c8(R[5][:, 0:T]), c8(R[5][:, 0:T]), R8[2][:, :].unsqueeze(2).to_broadcast([4, 8, 128]), AD)
            tt(R8[1][:, :], R8[2][:, :], mp[:, :], AD)
            tt(R8[3][:, :], lf[:, T:N], M0[:, :], AD)
            tt(R8[2][:, :], R8[3][:, :], li[:, T:N], ALU.max)
            L(nc.vector.tensor_copy(MOUT[:, 0:1], m[:, T - 1:T]))
            L(nc.vector.tensor_copy(MOUT[:, 1:9], R8[2][:, :]))
            tt(R8[3][:, :], R8[3][:, :], R8[2][:, :], SU_)
            nc.vector.tensor_tensor(R8[4][:, :], li[:, T:N], R8[2][:, :], SU_).then_inc(ml_e, 1)
            dve.wait_ge(ml_e, 1)
            dve_project(dve, SL_MKV + 4, 4)
            dve.wait_ge(ml_ej, 1)
            L(nc.vector.tensor_copy(BCOL[:, :, :], ps[:, 0, 64:96].rearrange("p (c h) -> p c h", h=4)))
            L(nc.vector.tensor_copy(EMCOL[:, :, :], ps[:, 0, 32:64].rearrange("p (c h) -> p c h", h=4)))
            nc.vector.tensor_copy(ECOL[:, :, :], ps[:, 0, 0:32].rearrange("p (c h) -> p c h", h=4)).then_inc(ml_ecol, 1)
            dve.wait_ge(ml_ecol, 1)
            L(nc.vector.memset(V1[:, :, 128:256], 1.0))
            L(nc.vector.memset(CC[:, 0, :], 0.0))
            for h in range(4):
                dve.wait_ge(ml_pe, ml_at("tr", h + 1))
                nc.vector.tensor_tensor(KE[:, :, :], two(2), ECOL[:, :, h:h + 1].to_broadcast([128, 8, 128]),
                                        M).then_inc(ml_dve, 1)
                dve.wait_ge(ml_exp, NCH * (h + 1))
                nc.vector.tensor_tensor(ST[:, :, :], c8(TMP[:, 0, 0:T]), two(6), M).then_inc(ml_dve, 1)
                dve.wait_ge(ml_dve, ml_did("st", h + 1))
                dve.wait_ge(ml_pe, ml_at("ab", h + 1))
                L(nc.vector.tensor_tensor(QA[:, :, :], c8(MQT[:, h, 0:T]), two(0), M))
                dve.wait_ge(ml_ebo, h + 1)
                dve.wait_ge(ml_pe, ml_at("dc", h + 1))
                if h:
                    dve.wait_ge(ml_out, 32 * h)
                for c in range(NCH):
                    ins = nc.vector.scalar_tensor_tensor(out=CC[:, c + 1, :], in0=CC[:, c, :], scalar=EB[:, 3, c:c + 1],
                                                         in1=ps[:, 4 + c // 2, (c % 2) * 256:(c % 2) * 256 + 256],
                                                         op0=M, op1=AD)
                    if c < NCH - 1:
                        L(ins)
                ins.then_inc(ml_dve, 1)
                tt(KS[:, :], MKT[:, h, T:N], EB[:, 1, :], M)
                tt(NS[:, h, :], NS[:, h, :], EB[:, 0, :], M)
                tt(NS[:, h, :], NS[:, h, :], KS[:, :], AD)
                nc.vector.tensor_tensor(QN[:, :], NS[:, h, :], MQT[:, h, T:N], M).then_inc(ml_dve, 1)
                dve.wait_ge(ml_pe, ml_at("nd", h + 1))
                nd = ps[:, 0:4, :].rearrange("p a (c i) -> p (a c) i", i=256)
                L(nc.vector.tensor_copy(DEN[:, 1, :], nd[:, :, 128]))
                L(nc.vector.scalar_tensor_tensor(out=DEN[:, 0, :], in0=DEN[:, 1, :], scalar=-1.0, in1=DEN[:, 1, :],
                                                 op0=M, op1=ALU.max))
                tt(DEN[:, 0, :], DEN[:, 0, :], EMCOL[:, :, h], ALU.max)
                L(nc.vector.reciprocal(DEN[:, 0, :], DEN[:, 0, :]))
                nc.vector.tensor_tensor(KE[:, :, :], nd[:, :, 0:128], DEN[:, 0, :].unsqueeze(2).to_broadcast([128, 8, 128]),
                                        M).then_inc(ml_dve, 1)
                dve.wait_ge(ml_pe, ml_at("st8", h + 1))
                dve.wait_ge(ml_kst, h + 1)
                nc.vector.tensor_tensor(VD[:, :, :], ps[0:8, 6, 128:256].unsqueeze(1).to_broadcast([8, 8, 128]),
                                        IDENT[0:8, 0:8].unsqueeze(2).to_broadcast([8, 8, 128]), M).then_inc(ml_dve, 1)
                dve.wait_ge(ml_sq, h + 1)
                nc.vector.tensor_reduce(DEN[:, 1, :], c8(TMP[:, 0, 0:T]), AX.X, AD).then_inc(ml_dve, 1)
                dve.wait_ge(ml_rt, h + 1)
                L(nc.vector.reciprocal(DEN[:, 2, :], DEN[:, 2, :]))
                nc.vector.tensor_tensor(KE[:, :, :], KE[:, :, :], DEN[:, 2, :].unsqueeze(2).to_broadcast([128, 8, 128]),
                                        M).then_inc(ml_dve, 1)
                dve.wait_ge(ml_cs_in, 16 * h + 16)
                tt(CS[:, :, :], CS[:, :, :], EB[:, 0, :].unsqueeze(2).to_broadcast([128, 8, 128]), M)
                dve.wait_ge(ml_pe, ml_at("kv", h + 1))
                nc.vector.tensor_tensor(CS[:, :, :], CS[:, :, :], two(6), AD).then_inc(ml_dve, 1)
                dve.wait_ge(ml_abs8, h + 1)
                tt(RS8[:, :], RS8[:, :], EB[:, 2, :], ALU.max)
                L(nc.vector.reciprocal(RS8[:, :], RS8[:, :]))
                nc.vector.tensor_tensor(MQT[:, h, T:N], RS8[:, :], ps[:, 4, 0:8], M).then_inc(ml_dve, 1)
                dve.wait_ge(ml_dve, ml_did("qn", h + 1))

        def pe_mlstm(pe):
            pe_project(pe, SL_MQ, G_MQ, 4)
            pe_project(pe, SL_MKV, G_MKV, 8)
            evacuated(pe, G_MKV + 8)
            pe.wait_ge(ml_rows, 7)
            for c in range(NCH):
                pe.transpose(ps[:, 0, 4 * c:4 * c + 4], R[5][:, chunk(c)], IDENT[0:4, 0:4])
                pe.transpose(ps[:, 0, 32 + 4 * c:36 + 4 * c], R[4][:, chunk(c)], IDENT[0:4, 0:4])
                last = pe.transpose(ps[:, 0, 64 + 4 * c:68 + 4 * c], R[1][:, chunk(c)], IDENT[0:4, 0:4])
            last.then_inc(ml_ej, 1)
            pe.wait_ge(ml_ecol, 1)
            for h in range(4):
                if h:
                    pe.wait_ge(ml_on, h)
                for c in range(NCH):
                    pe.transpose(two(0)[:, c, :], MVT[:, h, chunk(c)], IDENT)
                    last = pe.transpose(two(2)[:, c, :], MKT[:, h, chunk(c)], IDENT)
                last.then_inc(ml_pe, 1)
                if h:
                    pe.wait_ge(ml_dve, ml_did("qn", h))
                for k in range(2):
                    pe.matmul(ps[:, 4 + k, :], spread(h), ROWS[:, 512 * k:512 * k + 512], start=True, stop=False)
                    pe.matmul(ps[:, 4 + k, :].rearrange("p (c i) -> p c i", i=128), IDENT,
                              MASKNEG.unsqueeze(1).to_broadcast([128, 4, 128]), start=False, stop=True)
                for c in range(NCH):
                    last = pe.matmul(two(6)[:, c, :], MKT[:, h, chunk(c)], MQT[:, h, chunk(c)], start=True, stop=True)
                last.then_inc(ml_pe, 1)
                pe.wait_ge(ml_v, h + 1)
                for k in range(2):
                    last = pe.matmul(ps[:, k, :], spread(64 + h), ROWS[:, 512 * k:512 * k + 512], start=True, stop=True)
                last.then_inc(ml_pe, 1)
                pe.wait_ge(ml_dve, ml_did("ke", h + 1))
                for k, row in enumerate((0, 32, 96, 64)):
                    last = pe.matmul(ps[:, 2, 8 * k:8 * k + 8], spread(row + h), ROWS[:, T:N], start=True, stop=True)
                last.then_inc(ml_pe, 1)
                pe.wait_ge(ml_dve, ml_did("st", h + 1))
                for c in range(NCH):
                    last = pe.matmul(ps[:, 4 + c // 2, (c % 2) * 256:(c % 2) * 256 + 256], KE[:, c, :], V1[:, c, :],
                                     start=True, stop=True)
                last.then_inc(ml_pe, 1)
                pe.wait_ge(ml_dve, ml_did("c", h + 1))
                pe.wait_ge(ml_ebo, h + 1)
                for c in range(NCH):
                    out = ps[:, c // 2, (c % 2) * 256:(c % 2) * 256 + 129]
                    pe.matmul(out, ST[:, c, :], V1[:, c, 0:129], start=True, stop=False)
                    last = pe.matmul(out, QA[:, c, :], CC[:, c, 0:129], start=False, stop=True)
                last.then_inc(ml_pe, 1)
                pe.wait_ge(ml_dve, ml_did("ks", h + 1))
                pe.transpose(ps[0:8, 6, 0:128], KS[:, :], IDENT)
                pe.transpose(ps[0:8, 6, 128:256], MVT[:, h, T:N], IDENT).then_inc(ml_pe, 1)
                pe.wait_ge(ml_dve, ml_did("vd", h + 1))
                pe.wait_ge(ml_kst, h + 1)
                for k in range(2):
                    last = pe.matmul(ps[:, 6 + k, :], KST[:, :], VD[:, 4 * k:4 * k + 4, :].rearrange("p b v -> p (b v)"),
                                     start=True, stop=True)
                last.then_inc(ml_pe, 1)
                pe.wait_ge(ml_dve, ml_did("o", h + 1))
                for c in range(NCH):
                    last = pe.transpose(two(0)[:, c, :], KE[:, c, :], IDENT)
                last.then_inc(ml_pe, 1)
                pe.wait_ge(ml_dve, ml_did("cn", h + 1))
                for b_ in range(B):
                    pe.matmul(ps[:, 4, b_:b_ + 1], CS[:, b_, :], MQT[:, h, T + b_:T + b_ + 1], start=True, stop=True)
                pe.matmul(ps[:, 5, 8:16], ONES, QN[:, :], start=True, stop=True).then_inc(ml_pe, 1)

        def gated(m0_g, sl, base_m, func, tiles):
            def act_part(act):
                for m in range(4):
                    n, g = sl + m, m0_g + m
                    act.wait_ge(acc_ready, g + 1)
                    if m >= 2:
                        act.wait_ge(ml_y, base_m + m - 1)
                    nc.scalar.activation(t3(TMP[:, m % 2, :]), acc(g % 2), func).then_inc(ml_gate, 1)
                    act_hi(act, n + 2, n % 2, 16 * (n // 2 + 2), None)

            def dve_part(dve):
                for m in range(4):
                    dve.wait_ge(ml_gate, base_m + m + 1)
                    dve.sem_inc(acc_free[(m0_g + m) % 2], 1)
                    nc.vector.tensor_tensor(tiles[:, m, :], tiles[:, m, :], TMP[:, m % 2, :], ALU.mult).then_inc(ml_y, 1)
                    dve_lo(dve, sl + m + 2, (sl + m) % 2)
            return act_part, dve_part

        mo_act, mo_dve = gated(G_MO, SL_MO, 0, ACT.Sigmoid, MQT)

        def pool_store_yb(pool):
            pool.wait_ge(ml_y, 4)
            pool.dma_start(I["yb"], MQT).then_inc(yb_stored, 16)

        GQ = area("GQ", [128, 2 * N], 0)
        GKV = area("GKV", [128, 6 * N], 2 * N)
        GQT = GQ[:, :].rearrange("p (h n) -> p h n", n=N)
        GKT = GKV[:, 0:2 * N].rearrange("p (h n) -> p h n", n=N)
        GVT = GKV[:, 2 * N:6 * N].rearrange("p (h n) -> p h n", n=N)
        pos[0] = 8 * N
        GB = nxt("GB", [128, 2, N])
        QT, KTL = nxt("QT", [128, T]), nxt("KTL", [128, T])
        ATT = nxt("ATT", [128, 16, 128])
        VTOK = nxt("VTOK", [128, 16, 128])
        KD = nxt("KD", [128, NCH, 128])
        SZ = nxt("SZ", [128, NCH + 1, 2, 128])
        GS = nxt("GS", [128, B, 128])
        GVD = nxt("GVD", [8, 8, 128])
        KZ = nxt("KZ", [8, 2, 128])
        QZ = nxt("QZ", [128, B, 2])
        EG = nxt("EG", [128, 16])
        AX_ = (TMP[:, 0, :], RB[:, :])
        GMS = nxt("GMS", [128, 16])
        gl_a, gl_x, gl_abs, gl_ln, gl_b = sem("gl_a"), sem("gl_x"), sem("gl_abs"), sem("gl_ln"), sem("gl_b")
        gl_kdx, gl_kde, gl_kd, gl_tr, gl_v, gl_kdt = (sem("gl_kdx"), sem("gl_kde"), sem("gl_kd"), sem("gl_tr"),
                                                       sem("gl_v"), sem("gl_kdt"))
        gl_ds, gl_eg, gl_sz, gl_d, gl_e, gl_qk = (sem("gl_ds"), sem("gl_eg"), sem("gl_sz"), sem("gl_d"),
                                                   sem("gl_e"), sem("gl_qk"))
        gl_p, gl_att, gl_qe, gl_qe2, gl_o, gl_oo = (sem("gl_p"), sem("gl_att"), sem("gl_qe"), sem("gl_qe2"),
                                                     sem("gl_o"), sem("gl_oo"))
        gl_gs, gl_kt8, gl_kz, gl_vd, gl_kv = sem("gl_gs"), sem("gl_kt8"), sem("gl_kz"), sem("gl_vd"), sem("gl_kv")
        gl_osq, gl_ms, gl_rt, gl_on, gl_ot = sem("gl_osq"), sem("gl_ms"), sem("gl_rt"), sem("gl_on"), sem("gl_ot")
        gl_sn, gl_os, gl_oso, gl_out = sem("gl_sn"), sem("gl_os"), sem("gl_oso"), sem("gl_out")

        def four(k):
            return ps[:, k:k + 4, :].rearrange("p a (c i) -> p (a c) i", i=128)

        def pool_gla(pool):
            pool.wait_ge(ml_out, 160)
            pool.wait_ge(hn_done, 4)
            for hp in range(2):
                if hp:
                    pool.wait_ge(gl_out, 32 * hp)
                    pool.wait_ge(gl_os, hp)
                pool.dma_start(GS[:, :, :], I["gs0"][hp]).then_inc(gl_gs, 16)
                pool.wait_ge(gl_sn, hp + 1)
                pool.dma_start(O["gs_s"][hp], GS[:, :, :]).then_inc(gl_out, 16)
                pool.wait_ge(gl_sz, 8 * hp + 8)
                pool.dma_start(O["gs_p"][hp], SZ[:, NCH, :, :]).then_inc(gl_out, 16)

        def act_gla(act, st):
            act.wait_ge(ml_y, 4)
            for hp in range(2):
                act.wait_ge(gl_a, hp + 1)
                nc.scalar.activation(t3(AX_[hp]), acc(hp), ACT.Identity, bias=BALPHA[:, hp:hp + 1]).then_inc(gl_x, 1)

            def log_part(hp):
                act.wait_ge(gl_abs, hp + 1)
                st.link(nc.scalar.activation(TMP[:, 1, :], TMP[:, 1, :], ACT.Exp, scale=-1.0))
                nc.scalar.activation(TMP[:, 1, :], TMP[:, 1, :], ACT.Ln, bias=1.0).then_inc(gl_ln, 1)

            act.wait_ge(yb_stored, 16)
            act_project(act, SL_GQ, G_GQ, 2, GQ, 0, scale=64.0 ** -0.5)
            log_part(0)
            act_project(act, SL_GKV, G_GKV, 2, GKV, 0)
            log_part(1)
            act_project(act, SL_GKV + 2, G_GKV + 2, 4, GKV, 2)
            for hp in range(2):
                act.wait_ge(gl_kdx, hp + 1)
                nc.scalar.activation(QT[:, :], QT[:, :], ACT.Exp).then_inc(gl_kde, 1)
                ends = GB[:, hp, 0:T].rearrange("p (c i) -> p c i", i=128)[:, :, 127]
                nc.scalar.activation(EG[:, 0:8], ends, ACT.Exp).then_inc(gl_eg, 1)
                nc.scalar.activation(EG[:, 8:16], GB[:, hp, T:N], ACT.Exp).then_inc(gl_eg, 1)
                act.wait_ge(gl_tr, hp + 1)
                nc.scalar.activation(VTOK[:, :, :], ps[:, 0:4, :].rearrange("p a (c i) -> p (a c) i", i=128),
                                     ACT.Copy).then_inc(gl_v, 1)
                nc.scalar.activation(KD[:, :, :], two(4), ACT.Copy).then_inc(gl_kdt, 1)
                for l in range(1, LEVELS):
                    act.wait_ge(gl_d, (LEVELS - 1) * hp + l)
                    q_, k_ = (QT[:, :], KTL[:, :]) if l % 2 else (TMP[:, 0, 0:T], TMP[:, 1, 0:T])
                    q_, k_ = halves(q_, l), halves(k_, l)
                    nc.scalar.activation(q_[:, :, 1, :], q_[:, :, 1, :], ACT.Exp).then_inc(gl_e, 1)
                    nc.scalar.activation(k_[:, :, 0, :], k_[:, :, 0, :], ACT.Exp).then_inc(gl_e, 1)
                act.wait_ge(gl_p, LEVELS * hp + LEVELS)
                nc.scalar.activation(QT[:, :], GB[:, hp, 0:T], ACT.Exp).then_inc(gl_qe, 1)
                act.wait_ge(gl_o, hp + 1)
                nc.scalar.activation(ATT[:, :, :], four(0), ACT.Square).then_inc(gl_osq, 1)
                act.wait_ge(gl_ms, hp + 1)
                nc.scalar.activation(GMS[:, :], GMS[:, :], ACT.Sqrt, bias=EPSC, scale=1.0 / 128).then_inc(gl_rt, 1)
                act.wait_ge(gl_ot, hp + 1)
                for h2 in range(2):
                    nc.scalar.activation(GVT[:, 2 * hp + h2, 0:T].rearrange("p (c i) -> p c i", i=128),
                                         two(2 * h2), ACT.Copy, scale=GLAN[:, 2 * hp + h2:2 * hp + h2 + 1]).then_inc(gl_oo, 1)
                act.wait_ge(gl_os, hp + 1)
                nc.scalar.activation(GVT[:, 2 * hp:2 * hp + 2, T:N], ps[:, 4, 0:16].rearrange("p (b h) -> p h b", h=2),
                                     ACT.Copy).then_inc(gl_oso, 1)

        def halves(x, l):
            return x.rearrange("p (g a i) -> p g a i", a=2, i=1 << (l - 1))

        def dve_gla(dve, st):
            L = st.link
            M, AD, SU_ = ALU.mult, ALU.add, ALU.subtract
            tt = lambda o_, a, b_, op: L(nc.vector.tensor_tensor(o_, a, b_, op))

            def magnitude(hp):
                dve.wait_ge(gl_x, 2)
                nc.vector.scalar_tensor_tensor(out=TMP[:, 1, :], in0=AX_[hp], scalar=-1.0, in1=AX_[hp],
                                               op0=M, op1=ALU.max).then_inc(gl_abs, 1)

            def cumulate(hp):
                dve.wait_ge(gl_ln, hp + 1)
                L(nc.vector.scalar_tensor_tensor(out=AX_[hp], in0=AX_[hp], scalar=0.0, in1=TMP[:, 1, :],
                                                 op0=ALU.min, op1=SU_))
                L(nc.vector.tensor_scalar(AX_[hp], AX_[hp], 1.0 / 16.0, None, M))
                for c in range(NCH):
                    nc.vector.tensor_tensor_scan(GB[:, hp, chunk(c)], ONES[:, :], AX_[hp][:, chunk(c)], 0.0,
                                                 M, AD).then_inc(gl_b, 1)
                nc.vector.tensor_copy(GB[:, hp, T:N], AX_[hp][:, T:N]).then_inc(gl_b, 1)

            magnitude(0)
            dve_project(dve, SL_GQ, 2)
            cumulate(0)
            magnitude(1)
            dve_project(dve, SL_GKV, 2)
            cumulate(1)
            dve.wait_ge(gl_b, 18)
            dve_project(dve, SL_GKV + 2, 2)
            dve.wait_ge(ml_out, 160)
            L(nc.vector.memset(QT[:, :], 0.0))
            L(nc.vector.memset(KTL[:, :], 0.0))
            L(nc.vector.memset(SZ[:, :, :, :], 0.0))
            L(nc.vector.memset(KZ[:, :, :], 0.0))
            L(nc.vector.memset(QZ[:, :, :], 0.0))
            dve_project(dve, SL_GKV + 4, 2)
            for hp in range(2):
                gb = GB[:, hp, 0:T]
                c8 = lambda x: x.rearrange("p (c i) -> p c i", i=128)
                if hp:
                    dve.wait_ge(gl_o, hp)
                nc.vector.tensor_tensor(c8(QT[:, :]), c8(gb)[:, :, 127:128].to_broadcast([128, 8, 128]), c8(gb),
                                        SU_).then_inc(gl_kdx, 1)
                L(nc.vector.memset(ATT[:, :, :], 0.0))
                dve.wait_ge(gl_kde, hp + 1)
                nc.vector.tensor_tensor(QT[:, :], QT[:, :], GKT[:, hp, 0:T], M).then_inc(gl_kd, 1)
                dve.wait_ge(gl_eg, 2 * hp + 2)
                if hp:
                    dve.wait_ge(gl_out, 32 * hp)
                for h2 in range(2):
                    pr = slice(64 * h2, 64 * h2 + 64)
                    L(nc.vector.tensor_copy(QZ[pr, :, h2], GQT[pr, hp, T:N]))
                dve.wait_ge(gl_kt8, hp + 1)
                for h2 in range(2):
                    pr = slice(64 * h2, 64 * h2 + 64)
                    nc.vector.tensor_copy(KZ[:, h2, pr], ps[0:8, 6, 64 * h2:64 * h2 + 64]).then_inc(gl_kz, 1)
                for h2 in range(2):
                    if h2 or hp:
                        dve.wait_ge(gl_kv, 2 * hp + h2)
                    nc.vector.tensor_tensor(GVD[:, :, :],
                                            ps[0:8, 6, 128 + 128 * h2:256 + 128 * h2].unsqueeze(1).to_broadcast([8, 8, 128]),
                                            IDENT[0:8, 0:8].unsqueeze(2).to_broadcast([8, 8, 128]), M).then_inc(gl_vd, 1)
                dve.wait_ge(gl_gs, 16 * hp + 16)
                tt(GS[:, :, :], GS[:, :, :], EG[:, 8:16].unsqueeze(2).to_broadcast([128, 8, 128]), M)
                dve.wait_ge(gl_kv, 2 * hp + 2)
                nc.vector.tensor_tensor(GS[:, :, :], GS[:, :, :], two(4), AD).then_inc(gl_sn, 1)
                dve.wait_ge(gl_sn, hp + 1)
                dve.wait_ge(gl_ds, hp + 1)
                for c in range(NCH):
                    for h2 in range(2):
                        pr = slice(64 * h2, 64 * h2 + 64)
                        col = (c % 2) * 256 + 128 * h2
                        ins = nc.vector.scalar_tensor_tensor(out=SZ[pr, c + 1, h2, :], in0=SZ[pr, c, h2, :],
                                                             scalar=EG[pr, c:c + 1],
                                                             in1=ps[pr, c // 2, col:col + 128], op0=M, op1=AD)
                        if h2:
                            ins.then_inc(gl_sz, 1)
                            dve.wait_ge(gl_sz, 8 * hp + c + 1)
                for l in range(LEVELS):
                    n = LEVELS * hp + l
                    if l + 1 < LEVELS:
                        if l + 1 >= 3:
                            dve.wait_ge(gl_p, n)
                        q_, k_ = (QT[:, :], KTL[:, :]) if (l + 1) % 2 else (TMP[:, 0, 0:T], TMP[:, 1, 0:T])
                        q_, k_, g_ = halves(q_, l + 1), halves(k_, l + 1), halves(gb, l + 1)
                        w = 1 << l
                        ref = g_[:, :, 0, w - 1:w].to_broadcast([128, T // (2 * w), w])
                        L(nc.vector.tensor_tensor(q_[:, :, 1, :], g_[:, :, 1, :], ref, SU_))
                        nc.vector.tensor_tensor(k_[:, :, 0, :], ref, g_[:, :, 0, :], SU_).then_inc(gl_d, 1)
                        dve.wait_ge(gl_e, 2 * ((LEVELS - 1) * hp + l + 1))
                        qq, kk = halves(GQT[:, hp, 0:T], l + 1), halves(GKT[:, hp, 0:T], l + 1)
                        nc.vector.tensor_tensor(q_[:, :, 1, :], q_[:, :, 1, :], qq[:, :, 1, :], M).then_inc(gl_qk, 1)
                        nc.vector.tensor_tensor(k_[:, :, 0, :], k_[:, :, 0, :], kk[:, :, 0, :], M).then_inc(gl_qk, 1)
                    dve.wait_ge(gl_p, n + 1)
                    nc.vector.copy_predicated(ATT[:, :, :], LVL[:, l, :].unsqueeze(1).to_broadcast([128, 16, 128]),
                                              four(4 - 4 * (l % 2))
                                              ).then_inc(gl_att, 1)
                    dve.wait_ge(gl_att, n + 1)
                dve.wait_ge(gl_qe, hp + 1)
                nc.vector.tensor_tensor(QT[:, :], QT[:, :], GQT[:, hp, 0:T], M).then_inc(gl_qe2, 1)
                dve.wait_ge(gl_osq, hp + 1)
                nc.vector.tensor_reduce(GMS[:, :], ATT[:, :, :], AX.X, AD).then_inc(gl_ms, 1)
                dve.wait_ge(gl_rt, hp + 1)
                L(nc.vector.reciprocal(GMS[:, :], GMS[:, :]))
                nc.vector.tensor_tensor(VTOK[:, :, :], four(0), GMS[:, :].unsqueeze(2).to_broadcast([128, 16, 128]),
                                        M).then_inc(gl_on, 1)

        def pe_gla(pe):
            evacuated(pe, G_GQ)
            for hp in range(2):
                for t in range(NTG):
                    last = pe.matmul(banks(hp)[t], WALPHA[:, hp * 128:hp * 128 + 128], GT[0:16, t * TG:(t + 1) * TG],
                                     start=True, stop=True)
                last.then_inc(gl_a, 1)
            pe.wait_ge(gl_x, 2)
            pe_project(pe, SL_GQ, G_GQ, 2)
            pe_project(pe, SL_GKV, G_GKV, 6)
            evacuated(pe, G_GKV + 6)
            for hp in range(2):
                if hp:
                    pe.wait_ge(gl_oso, 1)
                for h2 in range(2):
                    for c in range(NCH):
                        pe.transpose(two(2 * h2)[:, c, :], GVT[:, 2 * hp + h2, chunk(c)], IDENT)
                pe.wait_ge(gl_kd, hp + 1)
                for c in range(NCH):
                    last = pe.transpose(two(4)[:, c, :], QT[:, chunk(c)], IDENT)
                last.then_inc(gl_tr, 1)
                pe.transpose(ps[0:8, 6, 0:128], GKT[:, hp, T:N], IDENT)
                for h2 in range(2):
                    last = pe.transpose(ps[0:8, 6, 128 + 128 * h2:256 + 128 * h2], GVT[:, 2 * hp + h2, T:N], IDENT)
                last.then_inc(gl_kt8, 1)
                pe.wait_ge(gl_kz, 2 * hp + 2)
                pe.wait_ge(gl_kdt, hp + 1)
                for h2 in range(2):
                    pe.wait_ge(gl_vd, 2 * hp + h2 + 1)
                    for k in range(2):
                        last = pe.matmul(ps[:, 4 + k, :], KZ[:, h2, :],
                                         GVD[:, 4 * k:4 * k + 4, :].rearrange("p b v -> p (b v)"),
                                         start=(h2 == 0), stop=(h2 == 1))
                    last.then_inc(gl_kv, 1)
                pe.wait_ge(gl_v, hp + 1)
                for c in range(NCH):
                    vt = VTOK[:, :, :].rearrange("p (h c) i -> p c h i", h=2)[:, c]
                    last = pe.matmul(ps[:, c // 2, (c % 2) * 256:(c % 2) * 256 + 256].rearrange("p (h i) -> p h i", h=2),
                                     KD[:, c, :], vt, start=True, stop=True)
                last.then_inc(gl_ds, 1)
                for l in range(LEVELS):
                    if l == 0:
                        q_, k_ = GQT[:, hp, 0:T], GKT[:, hp, 0:T]
                    else:
                        pe.wait_ge(gl_qk, 2 * ((LEVELS - 1) * hp + l))
                        q_, k_ = (QT[:, :], KTL[:, :]) if l % 2 else (TMP[:, 0, 0:T], TMP[:, 1, 0:T])
                    if l >= 2:
                        pe.wait_ge(gl_att, LEVELS * hp + l - 1)
                    elif l == 1:
                        pe.wait_ge(gl_sz, 8 * hp + 8)
                    else:
                        pe.wait_ge(gl_sn, hp + 1)
                    for h2 in range(2):
                        pr = slice(64 * h2, 64 * h2 + 64)
                        for c in range(NCH):
                            last = pe.matmul(two(4 - 4 * (l % 2) + 2 * h2)[:, c, :], k_[pr, chunk(c)], q_[pr, chunk(c)],
                                             start=True, stop=True)
                    last.then_inc(gl_p, 1)
                pe.wait_ge(gl_att, LEVELS * hp + LEVELS)
                pe.wait_ge(gl_qe2, hp + 1)
                for h2 in range(2):
                    for c in range(NCH):
                        pe.matmul(two(2 * h2)[:, c, :], ATT[:, h2 * 8 + c, :], VTOK[:, h2 * 8 + c, :],
                                  start=True, stop=False)
                        last = pe.matmul(two(2 * h2)[:, c, :], QT[:, chunk(c)], SZ[:, c, h2, :], start=False, stop=True)
                last.then_inc(gl_o, 1)
                for b_ in range(B):
                    last = pe.matmul(ps[:, 4, 2 * b_:2 * b_ + 2], GS[:, b_, :], QZ[:, b_, :], start=True, stop=True)
                last.then_inc(gl_os, 1)
                pe.wait_ge(gl_on, hp + 1)
                for c in range(16):
                    last = pe.transpose(four(0)[:, c, :], VTOK[:, c, :], IDENT)
                last.then_inc(gl_ot, 1)

        gr_act, gr_dve = gated(G_GR, SL_GR, 4, ACT.Silu, GVT)

        YH, YL = area("YH", [128, 4, N], 0, F32R), area("YL", [128, 4, N], 8 * N, F32R)
        RAW, MG = area("RAW", [128, 4, N], 4 * N), area("MG", [128, KT, N], 12 * N)
        XR = area("XR", [128, KT, N], 0)
        y_in, gate_slots, x_again = sem("y_in"), sem("gate_slots"), sem("x_again")
        yh_ready, yl_ready, merged = sem("yh_ready"), sem("yl_ready"), sem("merged")
        BRANCH = (GVT, RAW, RAW)

        def pool_gates(pool):
            for b, name in ((1, "yb"), (2, "yc")):
                pool.wait_ge(yl_ready, 4 * b)
                pool.dma_start(RAW[:], I[name]).then_inc(y_in, 16)
            pool.wait_ge(acc_ready, G_OUT)
            pool.dma_start(XR[:], I["xT"]).then_inc(x_again, 16)

        def pe_gates(pe):
            for b in range(3):
                with pe.Fori(0, 2) as i:
                    for p in range(2):
                        n, g = SL_GATE + 12 * b + 3 * p, G_GATE + 16 * b + 4 * p
                        for s in range(2):
                            pe.wait_ge(w_lo, i * 6 + (n + s + 1))
                            pe.wait_ge(acc_free[(g + s) % 2], i * 4 + (g + s) // 2)
                            split_product(pe, banks((g + s) % 2), (n + s) % 2, xh_cols, xl_cols, 0, KT).then_inc(acc_ready, 1)
                        pe.wait_ge(yl_ready, 4 * b + 4)
                        pe.wait_ge(w_lo, i * 6 + (n + 3))
                        for s in range(2):
                            pe.wait_ge(acc_free[(g + s) % 2], i * 4 + ((g + s) // 2 + 1))
                            split_product(pe, banks((g + s) % 2), (n + 2) % 2,
                                          lambda k, t: YH[:, k, t * TG:(t + 1) * TG],
                                          lambda k, t: YL[:, k, t * TG:(t + 1) * TG],
                                          4 * s, 4).then_inc(acc_ready, 1)

        def act_gates(act):
            act.wait_ge(ml_y, 8)
            act.wait_ge(gl_out, 64)
            for b in range(3):
                if b:
                    act.wait_ge(y_in, 16 * b)
                    act.wait_ge(acc_ready, G_GATE + 16 * b)
                for k in range(4):
                    nc.scalar.activation(YH[:, k, :], BRANCH[b][:, k, :], ACT.Copy).then_inc(yh_ready, 1)
                with act.Fori(0, 2) as i:
                    for p in range(2):
                        n, g = SL_GATE + 12 * b + 3 * p, G_GATE + 16 * b + 4 * p
                        for s in range(2):
                            act.wait_ge(acc_ready, i * 8 + (g + s + 1))
                            act.wait_ge(gate_slots, i * 4 + (8 * b + 2 * p + s + 1))
                            nc.scalar.activation(t3(TMP[:, s, :]), acc((g + s) % 2), ACT.Sigmoid).then_inc(
                                acc_free[(g + s) % 2], 1)
                            act_hi(act, None, (n + s) % 2, i * 48 + 16 * ((n + s) // 2 + 2), None)
                        act.wait_ge(acc_ready, i * 8 + (g + 4))
                        act_hi(act, None, n % 2, i * 48 + 16 * ((n + 2) // 2 + 2), None)

        def dve_gates(dve):
            dve.wait_ge(gl_out, 64)
            dve.sem_inc(gate_slots, 2)
            for b in range(3):
                for k in range(4):
                    dve.wait_ge(yh_ready, 4 * b + k + 1)
                    nc.vector.tensor_tensor(YL[:, k, :], BRANCH[b][:, k, :], YH[:, k, :].bitcast(F32),
                                            ALU.subtract).then_inc(yl_ready, 1)
                dve.wait_ge(gate_slots, 8 * b + 2)
                with dve.Fori(0, 2) as i:
                    for p in range(2):
                        n, g = SL_GATE + 12 * b + 3 * p, G_GATE + 16 * b + 4 * p
                        for s in range(2):
                            dve_lo(dve, i * 6 + (n + s + 2), (n + s) % 2)
                        for s in range(2):
                            a_, tmp = (g + s) % 2, TMP[:, s, :]
                            dve.wait_ge(acc_ready, i * 8 + (g + s + 3))
                            dve.wait_ge(acc_free[a_], i * 4 + ((g + s) // 2 + 1))
                            mg = MG[:, bass.ds(i * 4 + (2 * p + s), 1), :].rearrange("p a n -> p (a n)")
                            nc.vector.tensor_tensor(t3(tmp if b else mg), t3(tmp), acc(a_), ALU.mult).then_inc(acc_free[a_], 1)
                            dve.wait_ge(acc_free[a_], i * 4 + ((g + s) // 2 + 2))
                            if b:
                                nc.vector.tensor_tensor(mg, mg, tmp, ALU.add).then_inc(gate_slots, 1)
                            else:
                                dve.sem_inc(gate_slots, 1)
                        dve_lo(dve, i * 6 + (n + 4), n % 2)
            dve.wait_ge(gate_slots, 26)
            dve.sem_inc(merged, 1)

        def act_split(act, ks, src):
            for kt in range(KT):
                nc.scalar.activation(XH[:, kt, :], src[:, kt, :], ACT.Copy).then_inc(xh_ready, 1)

        def dve_split(dve, ks, src):
            for kt in range(KT):
                dve.wait_ge(xh_ready, KT * ks + kt + 1)
                nc.vector.tensor_tensor(XL[:, kt, :], src[:, kt, :], XH[:, kt, :].bitcast(F32),
                                        ALU.subtract).then_inc(xl_ready, 1)

        def act_prep_square(act, n0, g0, k):
            assert g0 % 2 == 1
            with act.Fori(0, KT // 2) as i:
                for s in range(2):
                    act.wait_ge(acc_free[(g0 + s) % 2], i + ((g0 + s) // 2 + 1))
                    act_square(act, i * 2 + (9 * k + s - 1), None,
                               XR[:, bass.ds(i * 2 + s, 1), :].rearrange("p a n -> p (a n)"), s, N)
                    act_hi(act, None, (n0 + s) % 2, i * 16 + 16 * ((n0 + s) // 2 + 2), None)

        def dve_residual(dve, st, n0, g0, k):
            st.link(nc.vector.memset(SS[:, :], 0.0))
            with dve.Fori(0, KT // 2) as i:
                for s in range(2):
                    g = g0 + s
                    dve.wait_ge(acc_ready, i * 2 + (g + 1))
                    x = XR[:, bass.ds(i * 2 + s, 1), :].rearrange("p a n -> p (a n)")
                    nc.vector.tensor_tensor(t3(x), t3(x), acc(g % 2), ALU.add).then_inc(acc_free[g % 2], 1)
                    dve_sum(dve, i * 2 + (KT * k + s), False, s, N, i * 2 + (9 * k + s))
                    dve_lo(dve, i * 2 + (n0 + s + 2), (n0 + s) % 2)

        def pe_out(pe):
            pe_first(pe, SL_OUT, G_OUT, 2)
            pe_project(pe, SL_OUT + 2, G_OUT + 2, KT - 2)

        def act_out(act):
            act.wait_ge(merged, 1)
            act.wait_ge(acc_ready, G_OUT)
            act_split(act, 2, MG)
            act_prep_square(act, SL_OUT, G_OUT, 2)

        def dve_out(dve, st):
            dve_split(dve, 2, MG)
            dve.wait_ge(x_again, 16)
            dve_residual(dve, st, SL_OUT, G_OUT, 2)

        QXF = area("QXF", [128, KT * N], 8 * N)
        QX = QXF[:, :].rearrange("p (k n) -> p k n", n=N)
        MK2, MV2 = area("MK2", [128, KT, MEM], 16 * N), area("MV2", [128, 2, D], 16 * N + 2048)
        SMX = area("SMX", [128, 4, 16], 16 * N + 4096)
        SM32 = area("SM32", [32, 4], 16 * N + 4160)
        S32 = area("S32", [32, MEM], 16 * N + 4168)
        DIA = (area("DIA0", [128, 32, 32], 16 * N + 4424), at("DIA1", [128, 32, 32], O_WPL))

        def diagonal(k):
            return DIA[k][:, :, :].rearrange("p a b -> p (a b)")[:, 0:1024:33]

        CACHE = at("CACHE", [128, B, 2048], O_XH)
        PA = (at("PA0", [128, 4, MEM], O_TMP), at("PA1", [128, 4, MEM], O_RB))
        PT = (at("PT0", [128, 4, 2, 128], O_TMP + N * 4), at("PT1", [128, 4, 2, 128], O_ROWS))
        mem_again, ck_in, cv_in = sem("mem_again"), [sem(f"ck_in{b}") for b in range(2)], [sem(f"cv_in{b}") for b in range(2)]
        x_s, x_max, x_exp, x_pn, x_t, x_tc, x_o, x_oc = (sem("x_s"), sem("x_max"), sem("x_exp"), sem("x_pn"),
                                                          sem("x_t"), sem("x_tc"), sem("x_o"), sem("x_oc"))
        y_s, y_q, y_max, y_exp, y_p = sem("y_s"), sem("y_q"), sem("y_max"), sem("y_exp"), sem("y_p")
        y_pt, y_pc, y_o, y_oc, y_ot = sem("y_pt"), sem("y_pc"), sem("y_o"), sem("y_oc"), sem("y_ot")

        HALF = 4

        def pool_cross(pool):
            pool.wait_ge(xl_ready, 3 * KT)
            pool.wait_ge(mem_kv_out, 32)
            pool.dma_start(MK2[:], O["mem_k"]).then_inc(mem_again, 16)
            pool.dma_start(MV2[:], O["mem_v"]).then_inc(mem_again, 16)
            pool.wait_ge(acc_ready, G_CQ + KT)
            for b in range(1, B, 2):
                pool.dma_start(CACHE[:, b], I["ck"][b]).then_inc(ck_in[1], 16)
            pool.wait_ge(y_s, 1)
            for b in range(1, B, 2):
                pool.dma_start(CACHE[:, b], I["cv"][b]).then_inc(cv_in[1], 16)

        def pe_cross(pe):
            pe_norm(pe, 2, N, G_OUT + KT)
            pe_first(pe, SL_CQ, G_CQ, 3)
            pe_project(pe, SL_CQ + 2, G_CQ + 2, KT - 2)
            evacuated(pe, G_CQ + KT)
            pe.wait_ge(mem_again, 32)

            def scores(t):
                if t >= 2:
                    pe.wait_ge(x_exp, 4 * (t - 1))
                b0 = (0, 6)[t % 2]
                for h in range(4):
                    out = ps[:, b0 + h // 2, (h % 2) * 256:(h % 2) * 256 + 256]
                    for dh in range(2):
                        last = pe.matmul(out, QX[:, 2 * h + dh, t * 128:t * 128 + 128], MK2[:, 2 * h + dh, :],
                                         start=(dh == 0), stop=(dh == 1))
                last.then_inc(x_s, 1)

            def tiles(lo, hi):
                scores(lo)
                for t in range(lo, hi):
                    if t + 1 < hi:
                        scores(t + 1)
                    pe.wait_ge(x_pn, t + 1)
                    if t:
                        pe.wait_ge(x_tc, t)
                    for h in range(4):
                        for mh in range(2):
                            last = pe.transpose(two(2)[:, 2 * h + mh, :], PA[t % 2][:, h, mh * 128:mh * 128 + 128], IDENT)
                    last.then_inc(x_t, 1)
                    pe.wait_ge(x_tc, t + 1)
                    if t:
                        pe.wait_ge(x_oc, t)
                    for h in range(4):
                        for dv in range(2):
                            for mh in range(2):
                                c = h * 256 + dv * 128
                                last = pe.matmul(two(4)[:, 2 * h + dv, :], MV2[:, mh, c:c + 128], PT[t % 2][:, h, mh, :],
                                                 start=(mh == 0), stop=(mh == 1))
                    last.then_inc(x_o, 1)

            tiles(0, HALF)
            for k in range(2):
                pe.wait_ge(ck_in[k], 64)
            pe.wait_ge(y_q, 2)
            for b in range(B):
                for h in range(4):
                    for dh in range(2):
                        c = (h * 2 + dh) * 256
                        last = pe.matmul(ps[0:32, 0, 0:256], DIA[dh][:, b * 4 + h, :], CACHE[:, b, c:c + 256],
                                         start=(b + h + dh == 0), stop=(b == B - 1 and h == 3 and dh == 1))
            last.then_inc(y_s, 1)
            pe.wait_ge(y_p, 1)
            for mh in range(2):
                last = pe.transpose(ps[:, 1, mh * 32:mh * 32 + 32], S32[:, mh * 128:mh * 128 + 128], IDENT[0:32, 0:32])
            last.then_inc(y_pt, 1)
            pe.wait_ge(y_pc, 2)
            tiles(HALF, 8)
            for k in range(2):
                pe.wait_ge(cv_in[k], 64)
            for b in range(B):
                for h in range(4):
                    for mh in range(2):
                        c = mh * D + h * 256
                        last = pe.matmul(ps[0:32, 0, 0:256], DIA[mh][:, b * 4 + h, :], CACHE[:, b, c:c + 256],
                                         start=(b + h + mh == 0), stop=(b == B - 1 and h == 3 and mh == 1))
            last.then_inc(y_o, 1)
            pe.wait_ge(y_oc, 1)
            for dv in range(2):
                last = pe.transpose(ps[:, 1, dv * 32:dv * 32 + 32], S32[:, dv * 128:dv * 128 + 128], IDENT[0:32, 0:32])
            last.then_inc(y_ot, 1)
            pe_first(pe, SL_CO, G_CO, 4)
            pe_project(pe, SL_CO + 2, G_CO + 2, KT - 2)

        def act_cross(act, st):
            act_norm(act, 2, 3, N, XH)
            act.wait_ge(mem_again, 32)
            act_project(act, SL_CQ, G_CQ, KT, QXF, 0, scale=256.0 ** -0.5)
            for b in range(0, B, 2):
                act.dma_start(CACHE[:, b], I["ck"][b]).then_inc(ck_in[0], 16)
            for t in range(8):
                if t == HALF:
                    act.wait_ge(y_s, 1)
                    for b in range(0, B, 2):
                        act.dma_start(CACHE[:, b], I["cv"][b]).then_inc(cv_in[0], 16)
                    act.wait_ge(y_max, 1)
                    nc.scalar.activation(S32[:, :], ps[0:32, 0, 0:256], ACT.Exp, bias=SM32[:, 0:1],
                                         accum_out=SM32[:, 1:2]).then_inc(y_exp, 1)
                    act.wait_ge(y_pt, 1)
                    for mh in range(2):
                        nc.scalar.activation(diagonal(mh), ps[:, 1, mh * 32:mh * 32 + 32], ACT.Copy).then_inc(y_pc, 1)
                act.wait_ge(x_max, t + 1)
                if t >= 2:
                    act.wait_ge(x_t, t - 1)
                b0 = (0, 6)[t % 2]
                for h in range(4):
                    nc.scalar.activation(PA[t % 2][:, h, :], ps[:, b0 + h // 2, (h % 2) * 256:(h % 2) * 256 + 256],
                                         ACT.Exp, bias=SMX[:, h, t % 2:t % 2 + 1],
                                         accum_out=SMX[:, h, 2 + t % 2:3 + t % 2]).then_inc(x_exp, 1)
                act.wait_ge(x_t, t + 1)
                if t >= 2:
                    act.wait_ge(x_o, t - 1)
                nc.scalar.activation(PT[t % 2][:, :, :, :].rearrange("p h m t -> p (h m) t"), two(2), ACT.Copy).then_inc(x_tc, 1)
                act.wait_ge(x_o, t + 1)
                nc.scalar.activation(QX[:, :, t * 128:t * 128 + 128], two(4), ACT.Copy).then_inc(x_oc, 1)
            act.wait_ge(y_o, 1)
            nc.scalar.activation(S32[:, :], ps[0:32, 0, 0:256], ACT.Copy).then_inc(y_oc, 1)
            act.wait_ge(y_ot, 1)
            for dv in range(2):
                nc.scalar.activation(QX[:, :, T:N].rearrange("p (h d) b -> p d h b", d=2)[:, dv],
                                     ps[:, 1, dv * 32:dv * 32 + 32].rearrange("p (b h) -> p h b", h=4),
                                     ACT.Copy).then_inc(y_oc, 1)
            act.wait_ge(y_oc, 3)
            act.wait_ge(x_oc, 8)
            act_split(act, 4, QX)
            act_prep_square(act, SL_CO, G_CO, 3)

        def dve_cross(dve, st):
            L = st.link
            dve_norm(dve, st, 2, 3, XR, 2, N, XH, XL)
            for k in range(2):
                L(nc.vector.memset(DIA[k][:, :, :], 0.0))
            dve_project(dve, SL_CQ, KT)
            dve.wait_ge(acc_free[(G_CQ + 7) % 2], (G_CQ + 7) // 2 + 1)
            dve.wait_ge(acc_free[(G_CQ + 6) % 2], (G_CQ + 6) // 2 + 1)
            for dh in range(2):
                nc.vector.tensor_copy(diagonal(dh).rearrange("p (b h) -> p b h", h=4),
                                      QX[:, :, T:N].rearrange("p (h d) b -> p d b h", d=2)[:, dh]).then_inc(y_q, 1)
            for t in range(8):
                if t == HALF:
                    dve.wait_ge(y_s, 1)
                    L(nc.vector.tensor_reduce(SM32[:, 2:3], ps[0:32, 0, 0:256], AX.X, ALU.max))
                    nc.vector.tensor_scalar(SM32[:, 0:1], SM32[:, 2:3], -1.0, None, ALU.mult).then_inc(y_max, 1)
                    dve.wait_ge(y_exp, 1)
                    L(nc.vector.reciprocal(SM32[:, 3:4], SM32[:, 1:2]))
                    nc.vector.tensor_scalar(S32[:, :], S32[:, :], SM32[:, 3:4], None, ALU.mult).then_inc(y_p, 1)
                b0 = (0, 6)[t % 2]
                dve.wait_ge(x_s, t + 1)
                L(nc.vector.tensor_reduce(SMX[:, :, 4 + t % 2], ps[:, b0:b0 + 2, :].rearrange("p a (h m) -> p (a h) m", m=256),
                                          AX.X, ALU.max))
                nc.vector.tensor_scalar(SMX[:, :, t % 2], SMX[:, :, 4 + t % 2], -1.0, None, ALU.mult).then_inc(x_max, 1)
                dve.wait_ge(x_exp, 4 * t + 4)
                L(nc.vector.reciprocal(SMX[:, :, 6 + t % 2], SMX[:, :, 2 + t % 2]))
                nc.vector.tensor_tensor(PA[t % 2][:, :, :], PA[t % 2][:, :, :],
                                        SMX[:, :, 6 + t % 2:7 + t % 2].to_broadcast([128, 4, MEM]), ALU.mult).then_inc(x_pn, 1)
            dve_split(dve, 4, QX)
            dve_residual(dve, st, SL_CO, G_CO, 3)

        HH = area("HH", [128, 2, 2, N], 8 * N, F32R)
        HL = area("HL", [128, 2, 2, N], 12 * N, F32R)
        UB = area("UB", [128, 2, N + 2], 16 * N)
        CA = area("CA", [128, 2, N], 16 * N + 2072)
        FW = area("FW", [128, 4 * 2 * NF], 16 * N + 2072 + 2 * N)
        FB = area("FB", [128, 2 * NF, 2, B], 16 * N + 2072 + 2 * N + 176)
        UPS = area("UPS", [128, 2 * NF, 10], 16 * N + 2072 + 2 * N + 176 + 704)
        ffn_in, u_slots, f_conv, f_silu, f_mul, f_hi, f_lo = (sem("ffn_in"), sem("u_slots"), sem("f_conv"),
                                                               sem("f_silu"), sem("f_mul"), sem("f_hi"), sem("f_lo"))
        y_ready, y_stored, f_stored = sem("y_ready"), sem("y_stored"), sem("f_stored")

        def pool_ffn(pool):
            pool.wait_ge(xl_ready, 5 * KT)
            pool.dma_start(FW[:], I["ffn_w"]).then_inc(ffn_in, 16)
            pool.dma_start(FB[:], I["ffn_buf"]).then_inc(ffn_in, 16)
            pool.dma_start(O["buf1"], I["buf1"]).then_inc(f_stored, 16)
            pool.wait_ge(u_slots, 2 * NF + 2)
            pool.dma_start(O["up_state"], UPS[:]).then_inc(f_stored, 16)
            pool.wait_ge(f_stored, 32)
            pool.wait_ge(mem_kv_out, 32)
            pool.wait_ge(s5_stored, 16)
            pool.wait_ge(ml_out, 160)
            pool.wait_ge(gl_out, 64)

        def pe_ffn(pe):
            pe_norm(pe, 3, N, G_CO + KT)

            def up(i, n, g, per_n, per_g, first=0):
                for k in range(first, 4):
                    pe.wait_ge(w_lo, i * per_n + (n + k + 1))
                    pe.wait_ge(acc_free[(g + k) % 2], i * (per_g // 2) + (g + k) // 2)
                    split_product(pe, banks((g + k) % 2), (n + k) % 2, xh_cols, xl_cols, 0, KT).then_inc(acc_ready, 1)

            def down(i, n, g, buf, h_need, per_n, per_g, per_h):
                pe.wait_ge(f_lo, i * per_h + h_need)
                for s in range(2):
                    pe.wait_ge(w_lo, i * per_n + (n + s + 1))
                    for m in range(4):
                        gg = g + 4 * s + m
                        pe.wait_ge(acc_free[gg % 2], i * (per_g // 2) + gg // 2)
                        split_product(pe, banks(gg % 2), (n + s) % 2,
                                      lambda k, t: HH[:, buf, k, t * TG:(t + 1) * TG],
                                      lambda k, t: HL[:, buf, k, t * TG:(t + 1) * TG],
                                      m, 2, 4).then_inc(acc_ready, 1)

            pe_first(pe, SL_FFN, G_FFN, 5)
            up(0, SL_FFN, G_FFN, 0, 0, 2)
            with pe.Fori(0, (NF // 2 - 1) // 2) as i:
                for c in range(2):
                    n, g = SL_FFN + 4 + 6 * c, G_FFN + 4 + 12 * c
                    up(i, n, g, 12, 24)
                    down(i, n + 4, g + 4, c, 2 * c + 2, 12, 24, 4)
            down(0, N_SLABS - 2, G_FFN + 124, 0, NF, 0, 0, 0)
            pe_norm(pe, 4, N, G_FFN + 132)

        def act_ffn(act, st):
            act_norm(act, 3, 5, N, XH)

            def silu(i, tile, k, per_t):
                act.wait_ge(f_conv, i * (per_t // 2) + ((tile + k) // 2 + 1))
                nc.scalar.activation(TMP[:, 0, :], CA[:, 1, :], ACT.Silu).then_inc(f_silu, 1)

            def product_hi(i, tile, k, buf, per_t):
                act.wait_ge(f_mul, i * (per_t // 2) + ((tile + k) // 2 + 1))
                nc.scalar.activation(HH[:, buf, k // 2, :], TMP[:, 1, :], ACT.Copy).then_inc(f_hi, 1)

            def up(i, n, g, tile, buf, per_n, per_g, per_t, whole):
                for k in range(4):
                    act.wait_ge(acc_ready, i * per_g + (g + k + 1))
                    act.wait_ge(u_slots, i * per_t + (tile + k + 1))
                    nc.scalar.activation(t3(UB[:, k % 2, 2:N + 2]), acc((g + k) % 2), ACT.Copy).then_inc(
                        acc_free[(g + k) % 2], 1)
                    act_hi(act, None, (n + k) % 2, i * (8 * per_n) + 16 * ((n + k) // 2 + 2), None)
                    if k == 1 or k == 3 and whole:
                        silu(i, tile, k, per_t)
                        product_hi(i, tile, k, buf, per_t)

            def down(i, n, g, tile, buf, per_n, per_g, per_t):
                silu(i, tile, 3, per_t)
                act.wait_ge(acc_ready, i * per_g + (g + 4))
                act_hi(act, None, n % 2, i * (8 * per_n) + 16 * (n // 2 + 2), None)
                product_hi(i, tile, 3, buf, per_t)
                act.wait_ge(acc_ready, i * per_g + (g + 8))
                act_hi(act, None, (n + 1) % 2, i * (8 * per_n) + 16 * ((n + 1) // 2 + 2), None)

            act.wait_ge(xl_ready, 6 * KT)
            up(0, SL_FFN, G_FFN, 0, 0, 0, 0, 0, True)
            with act.Fori(0, (NF // 2 - 1) // 2) as i:
                for c in range(2):
                    n, g = SL_FFN + 4 + 6 * c, G_FFN + 4 + 12 * c
                    up(i, n, g, 4 + 4 * c, (c + 1) % 2, 12, 24, 8, False)
                    down(i, n + 4, g + 4, 4 + 4 * c, (c + 1) % 2, 12, 24, 8)
            for m in range(KT):
                g = G_FFN + 124 + m
                act.wait_ge(acc_free[g % 2], g // 2 + 1)
                act_square(act, 36 + m - 1, None, XR[:, m, :], m % 2, N)
            act_norm(act, 4, 6, N)

        def dve_ffn(dve, st):
            L = st.link
            M, AD = ALU.mult, ALU.add
            dve_norm(dve, st, 3, 5, XR, 3, N, XH, XL)
            dve.wait_ge(ffn_in, 32)
            L(nc.vector.memset(UB[:, :, 0:2], 0.0))
            dve.sem_inc(u_slots, 2)

            def conv_row(i, c2, k, per_t):
                return i * (per_t // 2) + (c2 + k // 2 + (NF if k % 2 else 0))

            def conv_now(i, c2, k, per_t):
                w = [FW[:, bass.ds(conv_row(i, c2, k, per_t) * 4 + x, 1)] for x in range(4)]
                L(nc.vector.tensor_scalar(CA[:, k % 2, :], UB[:, k % 2, 2:N + 2], w[2], w[3], M, AD))

            def conv_one_back(i, c2, k, per_t):
                w = FW[:, bass.ds(conv_row(i, c2, k, per_t) * 4 + 1, 1)]
                c = CA[:, k % 2, 0:T]
                L(nc.vector.scalar_tensor_tensor(out=c, in0=UB[:, k % 2, 1:T + 1], scalar=w, in1=c, op0=M, op1=AD))

            def conv_two_back(i, c2, k, per_t):
                row = conv_row(i, c2, k, per_t)
                w = [FW[:, bass.ds(row * 4 + x, 1)] for x in range(2)]
                old = [FB[:, bass.ds(row, 1), x, :].rearrange("p a b -> p (a b)") for x in range(2)]
                c, u = CA[:, k % 2, :], UB[:, k % 2, :]
                L(nc.vector.scalar_tensor_tensor(out=c[:, 0:T], in0=u[:, 0:T], scalar=w[0], in1=c[:, 0:T], op0=M, op1=AD))
                L(nc.vector.scalar_tensor_tensor(out=c[:, T:N], in0=old[1], scalar=w[1], in1=c[:, T:N], op0=M, op1=AD))
                ins = nc.vector.scalar_tensor_tensor(out=c[:, T:N], in0=old[0], scalar=w[0], in1=c[:, T:N], op0=M, op1=AD)
                if k % 2:
                    ins.then_inc(f_conv, 1)
                else:
                    L(ins)
                nc.vector.tensor_copy(UPS[:, bass.ds(row, 1), :].rearrange("p a b -> p (a b)"), u[:, T:T + 10]).then_inc(u_slots, 1)

            def product(i, tile, k, per_t):
                dve.wait_ge(f_silu, i * (per_t // 2) + ((tile + k) // 2 + 1))
                nc.vector.tensor_tensor(TMP[:, 1, :], CA[:, 0, :], TMP[:, 0, :], M).then_inc(f_mul, 1)

            def product_lo(i, tile, k, buf, per_t):
                p = (tile + k) // 2 + 1
                dve.wait_ge(f_hi, i * (per_t // 2) + p)
                nc.vector.tensor_tensor(HL[:, buf, k // 2, :], TMP[:, 1, :], HH[:, buf, k // 2, :].bitcast(F32),
                                        ALU.subtract).then_inc(f_lo, 1)
                dve.wait_ge(f_lo, i * (per_t // 2) + p)

            def up(i, n, g, tile, c2, buf, per_n, per_g, per_t, whole):
                for k in range(4):
                    dve_lo(dve, i * per_n + (n + k + 2), (n + k) % 2)
                    dve.wait_ge(acc_free[(g + k) % 2], i * (per_g // 2) + ((g + k) // 2 + 1))
                    if k < 3 or whole:
                        conv_now(i, c2, k, per_t)
                        conv_one_back(i, c2, k, per_t)
                        conv_two_back(i, c2, k, per_t)
                    if k == 1 or k == 3 and whole:
                        product(i, tile, k, per_t)
                        product_lo(i, tile, k, buf, per_t)

            def down(i, n, g, tile, c2, buf, per_n, per_g, per_t):
                for m in range(8):
                    gg = g + m
                    dve.wait_ge(acc_ready, i * per_g + (gg + 1))
                    x = XR[:, m, :]
                    nc.vector.tensor_tensor(t3(x), t3(x), acc(gg % 2), AD).then_inc(acc_free[gg % 2], 1)
                    if m == 0:
                        conv_now(i, c2, 3, per_t)
                    elif m == 1:
                        conv_one_back(i, c2, 3, per_t)
                    elif m == 2:
                        conv_two_back(i, c2, 3, per_t)
                    elif m == 3:
                        dve_lo(dve, i * per_n + (n + 2), n % 2)
                    elif m == 4:
                        product(i, tile, 3, per_t)
                    elif m == 5:
                        product_lo(i, tile, 3, buf, per_t)
                dve_lo(dve, i * per_n + (n + 3), (n + 1) % 2)

            up(0, SL_FFN, G_FFN, 0, 0, 0, 0, 0, 0, True)
            per = 8 * 4 + 4
            with dve.Fori(0, (NF // 2 - 1) // 2) as i:
                st.enter(i, per)
                for c in range(2):
                    n, g = SL_FFN + 4 + 6 * c, G_FFN + 4 + 12 * c
                    up(i, n, g, 4 + 4 * c, 2 + 2 * c, (c + 1) % 2, 12, 24, 8, False)
                    down(i, n + 4, g + 4, 4 + 4 * c, 2 + 2 * c, (c + 1) % 2, 12, 24, 8)
                st.leave((NF // 2 - 1) // 2)
            L(nc.vector.memset(SS[:, :], 0.0))
            for m in range(KT):
                g = G_FFN + 124 + m
                dve.wait_ge(acc_ready, g + 1)
                x = XR[:, m, :]
                nc.vector.tensor_tensor(t3(x), t3(x), acc(g % 2), AD).then_inc(acc_free[g % 2], 1)
                dve_sum(dve, KT * 4 + m, False, m % 2, N, 36 + m)
            dve_norm_diag(dve, st, 4, N)
            for kt in range(KT):
                nc.vector.scalar_tensor_tensor(out=XR[:, kt, :], in0=XR[:, kt, :], scalar=GAIN[:, 4, kt:kt + 1],
                                               in1=RB[:, :], op0=M, op1=M).then_inc(y_ready, 1)

        def sp_final(sp):
            for kt in range(KT):
                sp.wait_ge(y_ready, kt + 1)
                sp.dma_start(O["y"][:, kt, :], XR[:, kt, :]).then_inc(y_stored, 16)
            sp.wait_ge(y_stored, 16 * KT)

        @block.sync
        def _(sp):
            sp_weights(sp)
            sp_final(sp)

        @block.gpsimd
        def _(pool):
            st = Steps(pool, pool_step)
            pool_load_first(pool)
            pool_s5_prepare(pool, st)
            pool_s5_tables(pool, st, 0)
            pool_store_mem(pool)
            pool_s5(pool, st)
            pool_glu(pool)
            pool_store_yc(pool)
            pool_mlstm(pool)
            pool_store_yb(pool)
            pool_gla(pool)
            pool_gates(pool)
            pool_cross(pool)
            pool_ffn(pool)

        @block.scalar
        def _(act):
            st = Steps(act, act_step)
            act_mem(act)
            act_mix_in(act)
            act_s5(act)
            act_glu(act)
            act_mlstm(act, st)
            act.wait_ge(ml_dve, ml_did("qn", 4))
            act_headnorm(act, 0, MQT)
            mo_act(act)
            act_gla(act, st)
            act.wait_ge(gl_oso, 2)
            act_headnorm(act, 1, GVT)
            gr_act(act)
            act_gates(act)
            act_out(act)
            act_cross(act, st)
            act_ffn(act, st)

        @block.vector
        def _(dve):
            st = Steps(dve, dve_step)
            dve_mem(dve, st)
            dve_mix_in(dve, st)
            dve_s5(dve, st)
            dve_glu(dve)
            dve_mlstm(dve, st)
            dve_headnorm(dve, st, 0, MQT, MLN)
            mo_dve(dve)
            dve_gla(dve, st)
            dve_headnorm(dve, st, 1, GVT, GLAN)
            gr_dve(dve)
            dve_gates(dve)
            dve_out(dve, st)
            dve_cross(dve, st)
            dve_ffn(dve, st)

        @block.tensor
        def _(pe):
            pe_mem(pe)
            pe_mix_in(pe)
            pe_s5(pe)
            pe_glu(pe)
            pe_mlstm(pe)
            pe_headnorm(pe, 0)
            pe.wait_ge(ml_on, 4)
            pe_project(pe, SL_MO, G_MO, 4)
            pe_gla(pe)
            pe.wait_ge(gl_oso, 2)
            pe_headnorm(pe, 1)
            pe.wait_ge(gl_oo, 4)
            pe_project(pe, SL_GR, G_GR, 4)
            pe_gates(pe)
            pe_out(pe)
            pe_cross(pe)
            pe_ffn(pe)


def lay_out(x):
    f = {k: np.asarray(v) for k, v in x.items()}
    z = np.zeros
    a = {}
    toks = np.concatenate([f["x_prompt"][0], f["x_sample"][:, 0]], 0)

    def feat(m):
        return m.T.reshape(KT, 128, -1).transpose(1, 0, 2)

    a["xT"] = feat(toks)
    a["memT"] = feat(f["mem_prompt"][0])

    def slabs(w):
        return w.reshape(KT, 128, -1, 128).transpose(2, 1, 0, 3)

    w_in = f["w_in"][0]
    sizes = (256, 256, 512, 512, 16, 512, 512, 512, 512, 4, 4, 512, D, D, D)
    names = ("gq", "gk", "gv", "gr", "ga", "mq", "mk", "mv", "mo", "mi", "mf", "su", "za", "zb", "zc")
    cut, pos_ = {}, 0
    for n_, s_ in zip(names, sizes):
        cut[n_] = w_in[:, pos_:pos_ + s_]
        pos_ += s_
    special = z((D, 128), np.float32)
    special[:, 0:16], special[:, 32:36], special[:, 64:68] = cut["ga"], cut["mi"], cut["mf"]

    def half(w):
        return w.reshape(4, 128, -1, 128).transpose(2, 1, 0, 3)

    gate = []
    for z_, w_ in (("za", "w_branch_a"), ("zb", "w_branch_b"), ("zc", "w_branch_c")):
        z_, w_ = slabs(cut[z_]), half(f[w_][0])
        for m in range(0, KT, 2):
            gate += [z_[m], z_[m + 1], np.concatenate([w_[m], w_[m + 1]], 1)]
    gate = np.stack(gate)
    up = slabs(f["w_ffn_up"][0])
    down = f["w_ffn_down"][0].reshape(NF // 2, 2, 128, 2, 4, 128).transpose(0, 3, 2, 1, 4, 5).reshape(NF // 2, 2, 128, 8, 128)
    ffn = [up[[0, NF, 1, NF + 1]]]
    for c in range(1, NF // 2):
        ffn += [up[[2 * c, NF + 2 * c, 2 * c + 1, NF + 2 * c + 1]], down[c - 1]]
    ffn += [down[NF // 2 - 1]]
    a["wslabs"] = np.concatenate([slabs(f["w_ck"][0]), slabs(f["w_cv"][0]), slabs(special), slabs(cut["su"]),
                                  slabs(cut["mq"]), slabs(cut["mk"]), slabs(cut["mv"]), slabs(cut["mo"]),
                                  slabs(cut["gq"]), slabs(cut["gk"]), slabs(cut["gv"]), slabs(cut["gr"]),
                                  gate, slabs(f["w_out"][0]), slabs(f["w_cq"][0]), slabs(f["w_co"][0])] + ffn, 0)

    a["wplain"] = half(f["s5_w_glu"][0])
    cf = z((128, 5, 128), np.float32)
    r = np.arange(128)
    cf[:, 0] = np.eye(128, dtype=np.float32)
    cf[:, 2] = np.where(r[:, None] <= r[None, :], np.float32(0), np.float32(NEG))
    cf[:, 3] = 1
    cf[64 + np.arange(64), 4, np.arange(64)] = -1
    cf[np.arange(64), 4, 64 + np.arange(64)] = 1
    a["cf"] = cf
    lvl = z((128, LEVELS, 128), np.float32)
    lvl[:, 0] = np.eye(128, dtype=np.float32)
    for l in range(1, LEVELS):
        h = 1 << (l - 1)
        same = (r[:, None] // (2 * h)) == (r[None, :] // (2 * h))
        lvl[:, l] = same & ((r[:, None] // h) % 2 == 0) & ((r[None, :] // h) % 2 == 1)
    a["lvl"] = lvl
    sc = z((128, 64), np.float32)

    def put(c, v, n_):
        sc[:, c:c + n_] = v.reshape(n_, 128).T

    for k, name in enumerate(("norm_mix", "norm_mem", "norm_cross", "norm_ffn")):
        put(8 * k, f[name][0], 8)
    put(32, f["norm_final"], 8)
    put(40, f["b_gla_alpha"][0], 2)
    put(42, f["gla_head_norm"][0], 4)
    put(46, f["mlstm_head_norm"][0], 4)
    put(50, f["s5_d"][0], 4)
    sc[:64, 54], sc[64:, 54], sc[:, 55] = 1, -1, EPS
    sc[:64, 57], sc[64:, 57] = -1, 1
    sc[32:36, 56], sc[64:68, 56] = f["b_mlstm_i"][0], f["b_mlstm_f"][0]
    a["sc"] = sc
    a["walpha"] = f["w_gla_alpha"][0]

    def twice(m):
        t = np.moveaxis(m, 1, 0)
        return np.concatenate([t, t], 0)

    def parts(p, q):
        p, q = np.moveaxis(p, 1, 0), np.moveaxis(q, 1, 0)
        return np.stack([np.concatenate([p, q], 0), np.concatenate([q, p], 0)], 1)

    ld = np.repeat(f["s5_log_dt"][0][:, None], 64, 1)
    a["s5par"] = np.stack([twice(f["s5_lam_re"][0]), twice(f["s5_lam_im"][0]), twice(ld)], 1)
    a["s5b"] = parts(f["s5_b_re"][0], f["s5_b_im"][0])
    a["s5c"] = parts(f["s5_c_re"][0].transpose(0, 2, 1), f["s5_c_im"][0].transpose(0, 2, 1))
    a["s5h0"] = parts(f["state_s5_re"][0].transpose(1, 2, 0), f["state_s5_im"][0].transpose(1, 2, 0))
    a["m0"] = f["state_mlstm_m"][0].T
    a["n0"] = f["state_mlstm_n"][0].transpose(2, 1, 0)
    a["c0"] = f["state_mlstm_c"][0].transpose(1, 2, 0, 3)
    a["gs0"] = f["state_gla"][0].reshape(B, 2, 128, 128).transpose(1, 2, 0, 3)
    a["ck"] = f["cache_mem_k"][0].reshape(B, MEM, 4, 2, 128).transpose(0, 4, 2, 3, 1).reshape(B, 128, 2048)
    a["cv"] = f["cache_mem_v"][0].reshape(B, 2, 128, D).transpose(0, 2, 1, 3).reshape(B, 128, 2048)
    fw = np.concatenate([f["ffn_conv_w"][0], f["ffn_conv_b"]], 0)
    a["ffn_w"] = fw.reshape(4, 2 * NF, 128).transpose(2, 1, 0).reshape(128, 8 * NF)
    buf = f["state_ffn_conv"][0]
    a["ffn_buf"] = buf.reshape(B, 2, 2 * NF, 128).transpose(3, 2, 1, 0)
    a["buf1"] = buf[:, 1].reshape(128, -1)
    return {k: np.ascontiguousarray(v) for k, v in a.items()}


_OUT = {"y": (128, KT, N), "mem_k": (128, KT, MEM), "mem_v": (128, 2, D), "s5_state": (128, 32, 9),
        "c_s": (4, 128, B, 128), "c_p": (4, 128, 129), "n_s": (128, 4, B), "m": (4, 9),
        "gs_s": (2, 128, B, 128), "gs_p": (2, 128, 2, 128), "up_state": (128, 2 * NF, 10),
        "buf1": (128, B * 2 * FF // 128)}


def tensors(nc, arrays):
    I = {k: nc.dram_tensor(f"in_{k}", v.shape, mybir.dt.from_np(v.dtype), kind="ExternalInput").ap()
         for k, v in arrays.items()}
    O = {k: nc.dram_tensor(f"out_{k}", s, F32, kind="ExternalOutput").ap() for k, s in _OUT.items()}
    for k in ("yb", "yc"):
        I[k] = nc.dram_tensor(f"scratch_{k}", (128, 4, N), F32, kind="Internal").ap()
    return I, O


def returned(r):
    y = r["y"].transpose(1, 0, 2).reshape(D, N).T
    y_p, y_s = y[None, :T], y[T:, None]
    gs = r["gs_p"]
    p_gla = np.stack([gs[h // 2, 64 * (h % 2):64 * (h % 2) + 64, h % 2] for h in range(4)])[None, None]
    p_c, p_n = r["c_p"][:, :, :128][None, None], r["c_p"][:, :, 128][None, None]
    p_m = r["m"][:, 0][None, None]
    s5 = r["s5_state"].reshape(2, 64, 32, 9)
    p_re, p_im = s5[0, :, :, 0].T[None, None], s5[1, :, :, 0].T[None, None]
    up = r["up_state"].transpose(2, 1, 0).reshape(10, 2 * FF)
    p_conv = up[None, None, 0:2]
    p_k = r["mem_k"].transpose(2, 1, 0).reshape(1, 1, MEM, 4, 256)
    p_v = r["mem_v"].transpose(1, 0, 2).reshape(1, 1, MEM, 4, 256)
    s_gla = r["gs_s"].transpose(2, 0, 1, 3).reshape(1, B, 4, 64, 128)
    s_c = r["c_s"].transpose(2, 0, 1, 3)[None]
    s_n = r["n_s"].transpose(2, 1, 0)[None]
    s_m = r["m"][:, 1:].T[None]
    s_re, s_im = s5[0, :, :, 1:].transpose(2, 1, 0)[None], s5[1, :, :, 1:].transpose(2, 1, 0)[None]
    s_conv = np.stack([r["buf1"].reshape(B, 2 * FF), up[2:]], 1)[None]
    out = (y_p, y_s, p_gla, p_c, p_n, p_m, p_re, p_im, p_conv, p_k, p_v, s_gla, s_c, s_n, s_m, s_re, s_im, s_conv)
    return tuple(np.ascontiguousarray(v) for v in out)


def kernel(**inputs):
    import concourse.bacc as bacc
    from concourse.bass_utils import run_bass_kernel_spmd as run

    arrays = lay_out(inputs)
    nc = bacc.Bacc("TRN2", target_bir_lowering=False, num_devices=1)
    I, O = tensors(nc, arrays)
    program(nc, I, O)
    r = run(nc, [{f"in_{k}": v for k, v in arrays.items()}], core_ids=[0]).results[0]
    return returned({k: r[f"out_{k}"] for k in _OUT})
```
